# Optimizing a Trainium2 kernel written in Bass

```python
import jax, jax.numpy as jnp
from jax import lax
import numpy as np

D_MODEL = 1024
BATCH = 1
SEQ = 128
DEPTH = 2
DEC_BATCH = 1
DEC_SEQ = 128
PAST_LEN = 128

GRID_W = 64
N_EVEN = (DEPTH + 1) // 2
N_ODD = DEPTH // 2

MLA_HEADS = 8
QK_NOPE = 64
QK_ROPE = 32
QK_HEAD = QK_NOPE + QK_ROPE
V_HEAD = 64
Q_LORA = 256
KV_LORA = 128
ROPE_THETA = 10000.0
MLA_WIDTH = MLA_HEADS * V_HEAD

SC_GROUPS = 8
SC_WIDTH = D_MODEL // 2
SC_KERNEL = 3

IN0_WIDTH = Q_LORA + KV_LORA + QK_ROPE + 3 * SC_WIDTH
IN0_SPLITS = (Q_LORA, Q_LORA + KV_LORA, Q_LORA + KV_LORA + QK_ROPE,
              Q_LORA + KV_LORA + QK_ROPE + SC_WIDTH, Q_LORA + KV_LORA + QK_ROPE + 2 * SC_WIDTH)

CONF_KERNEL = 31

D_FF = 2816
N_EXPERTS = 8
TOP_K = 2
D_FF_EXPERT = 3584

Q_BLOCK = 128
EPS = 1e-6

kernel_name = "hybrid_mla_shortconv_conformer_moe_dit_step"

def _rms(x, g):
    xf = x.astype(jnp.float32)
    y = xf * lax.rsqrt(jnp.mean(xf * xf, axis=-1, keepdims=True) + EPS)
    return (y * g.astype(jnp.float32)).astype(x.dtype)

def _layernorm(x, g, b):
    xf = x.astype(jnp.float32)
    mu = jnp.mean(xf, axis=-1, keepdims=True)
    var = jnp.mean(jnp.square(xf - mu), axis=-1, keepdims=True)
    y = (xf - mu) * lax.rsqrt(var + EPS)
    return (y * g.astype(jnp.float32) + b.astype(jnp.float32)).astype(x.dtype)

def _adaln(cond, w, b):
    m = jax.nn.silu(cond) @ w + b
    return [t[:, None, :] for t in jnp.split(m, 6, axis=-1)]

def _modulate(x, shift, scale):
    return x * (1.0 + scale) + shift

def _axial_rope(x):
    n = x.shape[1]
    rows = n // GRID_W
    row = jnp.repeat(jnp.arange(rows, dtype=jnp.float32), GRID_W)
    col = jnp.tile(jnp.arange(GRID_W, dtype=jnp.float32), rows)
    half = QK_ROPE // 2
    nf = half // 2
    inv = ROPE_THETA ** (-jnp.arange(nf, dtype=jnp.float32) / nf)

    def rot(xa, pos):
        ang = pos[:, None] * inv[None, :]
        ang = jnp.concatenate([ang, ang], axis=-1)[:, None, :]
        xf = xa.astype(jnp.float32)
        x1, x2 = xf[..., :nf], xf[..., nf:]
        return xf * jnp.cos(ang) + jnp.concatenate([-x2, x1], axis=-1) * jnp.sin(ang)

    out = jnp.concatenate([rot(x[..., :half], row), rot(x[..., half:], col)], axis=-1)
    return out.astype(x.dtype)

def _attend(q, k, v):
    b, h, nq, dh = q.shape
    nb = nq // Q_BLOCK
    qb = jnp.moveaxis(q.reshape(b, h, nb, Q_BLOCK, dh), 2, 0)

    def block(qi):
        s = jnp.einsum('bhqd,bhkd->bhqk', qi, k).astype(jnp.float32) * (QK_HEAD ** -0.5)
        p = jax.nn.softmax(s, axis=-1).astype(v.dtype)
        return jnp.einsum('bhqk,bhkv->bhqv', p, v)

    o = lax.map(block, qb)
    return jnp.moveaxis(o, 0, 2).reshape(b, h, nq, v.shape[-1])

def _short_conv(gb, gc, u, w):
    v = gc * u
    n = v.shape[1]
    pad = SC_KERNEL // 2
    vp = jnp.pad(v, ((0, 0), (pad, pad), (0, 0)))
    y = w[0] * vp[:, 0:n]
    for j in range(1, SC_KERNEL):
        y = y + w[j] * vp[:, j:j + n]
    return gb * y

def _even_project(h, p):
    z = h @ p["w_in"]
    q_lat, ckv, kpe, gb, gc, u = jnp.split(z, IN0_SPLITS, axis=-1)
    ckv = _rms(ckv, p["kv_a_norm"])
    return q_lat, ckv, kpe, gb, gc, u

def _mla_queries(q_lat, p, rope):
    b, n, _ = q_lat.shape
    q = (_rms(q_lat, p["q_a_norm"]) @ p["w_qb"]).reshape(b, n, MLA_HEADS, QK_HEAD)
    q = _rms(q, p["q_norm"])
    if rope:
        q = jnp.concatenate([q[..., :QK_NOPE], _axial_rope(q[..., QK_NOPE:])], axis=-1)
    return q.transpose(0, 2, 1, 3)

def _mla_keys_values(ckv, kpe, p, rope):
    b, n, _ = ckv.shape
    kv = (ckv @ p["w_kvb"]).reshape(b, n, MLA_HEADS, QK_NOPE + V_HEAD)
    k_nope, v = kv[..., :QK_NOPE], kv[..., QK_NOPE:]
    k_pe = jnp.broadcast_to(kpe[:, :, None, :], (b, n, MLA_HEADS, QK_ROPE))
    k = _rms(jnp.concatenate([k_nope, k_pe], axis=-1), p["k_norm"])
    if rope:
        k = jnp.concatenate([k[..., :QK_NOPE], _axial_rope(k[..., QK_NOPE:])], axis=-1)
    return k.transpose(0, 2, 1, 3), v.transpose(0, 2, 1, 3)

def _even_out(attn, sc, w_o):
    b, h, n, dv = attn.shape
    a = attn.transpose(0, 2, 1, 3).reshape(b, n, h * dv)
    return jnp.concatenate([a, sc], axis=-1) @ w_o

def _even_mixer_context(h, p):
    q_lat, ckv, kpe, gb, gc, u = _even_project(h, p)
    q = _mla_queries(q_lat, p, rope=False)
    k, v = _mla_keys_values(ckv, kpe, p, rope=False)
    out = _even_out(_attend(q, k, v), _short_conv(gb, gc, u, p["w_sc"]), p["w_o"])
    return out, ckv, kpe

def _even_mixer_latent(h, ckv_ctx, kpe_ctx, p):
    q_lat, ckv, kpe, gb, gc, u = _even_project(h, p)
    q = _mla_queries(q_lat, p, rope=True)
    k_lat, v_lat = _mla_keys_values(ckv, kpe, p, rope=True)
    k_ctx, v_ctx = _mla_keys_values(ckv_ctx, kpe_ctx, p, rope=False)
    k = jnp.concatenate([k_ctx, k_lat], axis=2)
    v = jnp.concatenate([v_ctx, v_lat], axis=2)
    return _even_out(_attend(q, k, v), _short_conv(gb, gc, u, p["w_sc"]), p["w_o"])

def _conformer_conv(h, p):
    z = h @ p["w_pw1"] + p["b_pw1"]
    a, g = jnp.split(z, 2, axis=-1)
    u = a * jax.nn.sigmoid(g)
    u = lax.conv_general_dilated(
        u, p["w_dw"][:, None, :], window_strides=(1,),
        padding=((CONF_KERNEL // 2, CONF_KERNEL // 2),),
        dimension_numbers=('NWC', 'WIO', 'NWC'),
        feature_group_count=u.shape[-1]) + p["b_dw"]
    u = jax.nn.silu(_layernorm(u, p["ln_g"], p["ln_b"]))
    return u @ p["w_pw2"] + p["b_pw2"]

def _swiglu(h, w_gu, w_down):
    g, u = jnp.split(h @ w_gu, 2, axis=-1)
    return (jax.nn.silu(g) * u) @ w_down

def _moe(h, router, w_gu, w_down):
    b, n, d = h.shape
    t = h.reshape(b * n, d)
    logits = (t @ router).astype(jnp.float32)
    top_v, top_i = lax.top_k(logits, TOP_K)
    w = jax.nn.softmax(top_v, axis=-1)
    gates = jnp.sum(jax.nn.one_hot(top_i, N_EXPERTS, dtype=jnp.float32) * w[..., None], axis=-2)
    out = jnp.zeros_like(t)
    for e in range(N_EXPERTS):
        out = out + gates[:, e:e + 1].astype(t.dtype) * _swiglu(t, w_gu[e], w_down[e])
    return out.reshape(b, n, d)

def setup_inputs(seed: int = 0) -> dict:
    key = jax.random.key(seed)
    kiter = iter(list(jax.random.split(key, 64)))
    D = D_MODEL

    def nrm(shape, scale):
        return scale * jax.random.normal(next(kiter), shape, jnp.float32)

    def gain(shape):
        return 1.0 + nrm(shape, 0.1)

    return {
        "x_prompt": nrm((BATCH, SEQ, D), 1.0),
        "x_sample": nrm((DEC_BATCH, DEC_SEQ, D), 1.0),
        "cache_ckv": nrm((DEC_BATCH, N_EVEN, PAST_LEN, KV_LORA), 1.0),
        "cache_kpe": nrm((DEC_BATCH, N_EVEN, PAST_LEN, QK_ROPE), 1.0),
        "c": nrm((DEC_BATCH, D), 1.0),
        "c_ctx": nrm((D,), 1.0),
        "ada_w": nrm((DEPTH, D, 6 * D), 0.5 * D ** -0.5),
        "ada_b": nrm((DEPTH, 6 * D), 0.02),
        "norm_mix": gain((DEPTH, D)),
        "norm_ffn": gain((DEPTH, D)),
        "w_in": nrm((N_EVEN, D, IN0_WIDTH), D ** -0.5),
        "q_a_norm": gain((N_EVEN, Q_LORA)),
        "w_qb": nrm((N_EVEN, Q_LORA, MLA_HEADS * QK_HEAD), Q_LORA ** -0.5),
        "kv_a_norm": gain((N_EVEN, KV_LORA)),
        "w_kvb": nrm((N_EVEN, KV_LORA, MLA_HEADS * (QK_NOPE + V_HEAD)), KV_LORA ** -0.5),
        "q_norm": gain((N_EVEN, QK_HEAD)),
        "k_norm": gain((N_EVEN, QK_HEAD)),
        "w_sc": nrm((N_EVEN, SC_KERNEL, SC_WIDTH), SC_KERNEL ** -0.5),
        "w_o": nrm((N_EVEN, MLA_WIDTH + SC_WIDTH, D), (MLA_WIDTH + SC_WIDTH) ** -0.5),
        "ffn_gu": nrm((N_EVEN, D, 2 * D_FF), D ** -0.5),
        "ffn_down": nrm((N_EVEN, D_FF, D), D_FF ** -0.5),
        "conv_pw1": nrm((N_ODD, D, 2 * D), D ** -0.5),
        "conv_pw1_b": nrm((N_ODD, 2 * D), 0.02),
        "conv_dw": nrm((N_ODD, CONF_KERNEL, D), CONF_KERNEL ** -0.5),
        "conv_dw_b": nrm((N_ODD, D), 0.02),
        "conv_ln_g": gain((N_ODD, D)),
        "conv_ln_b": nrm((N_ODD, D), 0.02),
        "conv_pw2": nrm((N_ODD, D, D), D ** -0.5),
        "conv_pw2_b": nrm((N_ODD, D), 0.02),
        "router": nrm((N_ODD, D, N_EXPERTS), D ** -0.5),
        "moe_gu": nrm((N_ODD, N_EXPERTS, D, 2 * D_FF_EXPERT), D ** -0.5),
        "moe_down": nrm((N_ODD, N_EXPERTS, D_FF_EXPERT, D), D_FF_EXPERT ** -0.5),
    }

def reference(x_prompt, x_sample, cache_ckv, cache_kpe, c, c_ctx,
              ada_w, ada_b, norm_mix, norm_ffn,
              w_in, q_a_norm, w_qb, kv_a_norm, w_kvb, q_norm, k_norm, w_sc, w_o,
              ffn_gu, ffn_down,
              conv_pw1, conv_pw1_b, conv_dw, conv_dw_b, conv_ln_g, conv_ln_b, conv_pw2, conv_pw2_b,
              router, moe_gu, moe_down):
    xp = x_prompt
    xs = x_sample
    new_ckv = []
    new_kpe = []
    for l in range(DEPTH):
        i = l // 2
        m_ctx = _adaln(c_ctx[None, :], ada_w[l], ada_b[l])
        m_lat = _adaln(c, ada_w[l], ada_b[l])
        hp = _modulate(_rms(xp, norm_mix[l]), m_ctx[0], m_ctx[1])
        hs = _modulate(_rms(xs, norm_mix[l]), m_lat[0], m_lat[1])
        if l % 2 == 0:
            p = dict(w_in=w_in[i], q_a_norm=q_a_norm[i], w_qb=w_qb[i], kv_a_norm=kv_a_norm[i],
                     w_kvb=w_kvb[i], q_norm=q_norm[i], k_norm=k_norm[i], w_sc=w_sc[i], w_o=w_o[i])
            op, ckv_p, kpe_p = _even_mixer_context(hp, p)
            os_ = _even_mixer_latent(hs, cache_ckv[:, i], cache_kpe[:, i], p)
            new_ckv.append(ckv_p)
            new_kpe.append(kpe_p)
        else:
            p = dict(w_pw1=conv_pw1[i], b_pw1=conv_pw1_b[i], w_dw=conv_dw[i], b_dw=conv_dw_b[i],
                     ln_g=conv_ln_g[i], ln_b=conv_ln_b[i], w_pw2=conv_pw2[i], b_pw2=conv_pw2_b[i])
            op = _conformer_conv(hp, p)
            os_ = _conformer_conv(hs, p)
        xp = xp + m_ctx[2] * op
        xs = xs + m_lat[2] * os_
        hp = _modulate(_rms(xp, norm_ffn[l]), m_ctx[3], m_ctx[4])
        hs = _modulate(_rms(xs, norm_ffn[l]), m_lat[3], m_lat[4])
        if l % 2 == 0:
            fp = _swiglu(hp, ffn_gu[i], ffn_down[i])
            fs = _swiglu(hs, ffn_gu[i], ffn_down[i])
        else:
            fp = _moe(hp, router[i], moe_gu[i], moe_down[i])
            fs = _moe(hs, router[i], moe_gu[i], moe_down[i])
        xp = xp + m_ctx[5] * fp
        xs = xs + m_lat[5] * fs
    state_ckv = jnp.stack(new_ckv, axis=1)
    state_kpe = jnp.stack(new_kpe, axis=1)
    return (xp, xs, state_ckv, state_kpe)


_drawn_inputs = setup_inputs


def setup_inputs(seed=0):
    import zlib

    import numpy as np

    out = dict(_drawn_inputs(seed))
    spreads = {}
    factors = {'cache_ckv': 3.279,
     'cache_kpe': 5.693,
     'q_a_norm': 5.862,
     'q_norm': 8.0,
     'k_norm': 8.0,
     'conv_pw1_b': 5.765,
     'conv_dw_b': 6.754,
     'conv_ln_b': 5.78,
     'conv_pw2_b': 8.0}
    for name, (base, spread) in spreads.items():
        noise = np.random.default_rng([zlib.crc32(name.encode()), seed]).standard_normal(out[name].shape)
        drawn = base * np.exp(spread * noise) if base else spread * noise
        out[name] = __import__('jax').numpy.asarray(drawn.astype(out[name].dtype))
    for name, factor in factors.items():
        out[name] = (out[name] * factor).astype(out[name].dtype)
    return out
```

```python
import concourse.bass as bass
from concourse import mybir
from contextlib import ExitStack

F32 = mybir.dt.float32
F32R = mybir.dt.float32r
I32 = mybir.dt.int32
ALU = mybir.AluOpType
ACT = mybir.ActivationFunctionType
AX = mybir.AxisListType.X

P = 128
D = 1024
KT = D // P
KH = KT // 2
TILES = 2
HEADS, NOPE, ROPE, VH = 8, 64, 32, 64
QK = NOPE + ROPE
Q_LORA, KV_LORA = 256, 128
SC = 512
SCC = SC // P
TAPS = 31
PAD = TAPS // 2
D_FF, D_FFE, EXPERTS = 2816, 3584, 8
UNIT = 256
UC = UNIT // P
EPS = 1e-6
SCALE = float(QK) ** -0.5
Z0 = Q_LORA + KV_LORA + ROPE
RAWS = 6
SPLITS = 3
PIECE = 2048

C_ID, C_BEFORE, C_ONES, C_IOTA = 0, P, 2 * P, 3 * P
C_COS = 4 * P
C_SIN = C_COS + HEADS * ROPE
C_SUM2 = C_SIN + HEADS * ROPE
C_SUMB = C_SUM2 + 2
C_END = C_SUMB + 2 * P

ROWS = {}
_r = 0
for _name, _n in (("c_ctx", 8), ("c", 8), ("norm_mix", 16), ("norm_ffn", 16), ("pw1_b", 16), ("dw_b", 8),
                  ("ln_g", 8), ("ln_b", 8), ("w_sc", 12), ("q_a", 2)):
    ROWS[_name] = _r
    _r += _n
NROWS = _r

ADA_FIRST = [(0, 2), (0, 3), (0, 0), (0, 1)]
ADA_ATTN = [(0, 8), (0, 9), (0, 6), (0, 7), (1, 2), (1, 3), (1, 0), (1, 1), (1, 8), (1, 9), (1, 6), (1, 7)]
ADA_GATE = [[(0, 4), (0, 5)], [(0, 10), (0, 11)], [(1, 4), (1, 5)], [(1, 10), (1, 11)]]


def ffn_stream(units):
    out = []
    for u in range(units):
        out += [("a", u), ("b", u)]
        if u >= 2:
            out.append(("d", u - 2))
    return out + [("d", units - 2), ("d", units - 1)]


def plan():
    order = []

    def ada(chunks):
        for c in chunks:
            order.extend([("ada", c, 0), ("ada", c, 1)])

    ada(ADA_FIRST)
    order.extend([("win", c, kh) for c in (0, 2) for kh in (0, 1)])
    order.extend([("qb",), ("kvb",)])
    order.extend([("win", c, kh) for c in (3, 1) for kh in (0, 1)])
    ada(ADA_ATTN)
    ada(ADA_GATE[0])
    order.extend([("wo", h, kh) for h in (0, 1) for kh in (0, 1)])
    ada(ADA_GATE[1])
    order.extend([("ffn", k, u) for k, u in ffn_stream(D_FF // UNIT)])
    ada(ADA_GATE[2])
    order.extend([("pw1", k, u) for u in range(4) for k in "ab"])
    order.extend([("pw2", h, kh) for h in (0, 1) for kh in (0, 1)])
    ada(ADA_GATE[3])
    return order, {p: n for n, p in enumerate(order)}


ORDER, NUM = plan()
N_DENSE = len(ORDER)
UNITS_E = D_FFE // UNIT
STREAM_E = ffn_stream(UNITS_E)
NUM_E = {p: n for n, p in enumerate(STREAM_E)}
PER_E = len(STREAM_E)
assert PER_E % RAWS == 0 and PER_E % SPLITS == 0
W_CHUNK = {0: (0, Z0), 1: (Z0, SC), 2: (Z0 + SC, SC), 3: (Z0 + 2 * SC, SC)}


def build(nc, t, outs):
    ctx = ExitStack()
    with ctx:
        def sb(name, shape, dt=F32, where=None):
            return (where or ctx).enter_context(nc.sbuf_tensor(name, shape, dt))

        raw = sb("raw", [P, RAWS, PIECE])
        high = sb("high", [P, SPLITS, PIECE], F32R)
        low = sb("low", [P, SPLITS, PIECE], F32R)
        x = sb("x", [P, TILES, D])
        hid = sb("hid", [P, KT, TILES * P])
        hidH = sb("hidH", [P, KT, TILES * P], F32R)
        hidL = sb("hidL", [P, KT, TILES * P], F32R)
        gate = sb("gate", [P, TILES, D])
        upH = sb("upH", [P, 2, UC, TILES * P], F32R)
        upL = sb("upL", [P, 2, UC, TILES * P], F32R)
        const = sb("const", [P, C_END])
        par = sb("par", [P, NROWS])
        ada_bT = sb("ada_bT", [P, 2 * 48])
        taps = sb("taps", [P, TAPS * KT])
        cH = sb("cH", [P, KT, 4], F32R)
        mod = sb("mod", [P, 2, 4, KT, 2])
        aff = sb("aff", [P, KT, 2])
        ada4 = sb("ada4", [4, 512])
        small = sb("small", [P, 64])
        router_w = sb("router_w", [P, KT, EXPERTS])
        ph = ExitStack()
        z0 = sb("z0", [P, TILES, Z0], where=ph)
        kv_lat = sb("kv_lat", [P, 3, KV_LORA], where=ph)
        kpe_c = sb("kpe_c", [P, ROPE], where=ph)
        kv_gain = sb("kv_gain", [P, KV_LORA], where=ph)
        q_gain = sb("q_gain", [P, QK], where=ph)
        k_gain = sb("k_gain", [P, QK], where=ph)
        vals = sb("vals", [P, 3, HEADS, VH], where=ph)
        qT = sb("qT", [QK, TILES, HEADS, P], where=ph)
        kT = sb("kT", [QK, 3, HEADS, P], where=ph)
        work = sb("work", [P, 3 * HEADS * P], where=ph)
        probT = sb("probT", [P, 2, 4, P], where=ph)
        rope_t = sb("rope_t", [P, HEADS, ROPE], where=ph)
        vTpad = sb("vTpad", [P, SCC, TILES, P + 2], where=ph)
        ph.close()
        ph = ExitStack()
        act = sb("act", [P, 2, TILES, UNIT], where=ph)
        ph.close()
        ph = ExitStack()
        ag = sb("ag", [P, 2, TILES, 512], where=ph)
        uT = sb("uT", [P, KT, TILES, P + 2 * PAD], where=ph)
        sg = sb("sg", [P, UC, TILES, P], where=ph)
        sq = sb("sq", [P, KT, TILES * P], where=ph)
        stat = sb("stat", [P, 2, TILES * P], where=ph)
        pw2_b = sb("pw2_b", [1, D], where=ph)
        ph.close()
        ph = ExitStack()
        tokH = sb("tokH", [P, TILES, D], F32R, where=ph)
        tokL = sb("tokL", [P, TILES, D], F32R, where=ph)
        slotH = sb("slotH", [P, KT, P], F32R, where=ph)
        slotL = sb("slotL", [P, KT, P], F32R, where=ph)
        outH = sb("outH", [P, D], F32R, where=ph)
        outL = sb("outL", [P, D], F32R, where=ph)
        eact = sb("eact", [P, 2, UNIT], where=ph)
        pick = sb("pick", [P, TILES, P], where=ph)
        pickR = sb("pickR", [P, TILES, P], F32R, where=ph)
        backR = sb("backR", [P, TILES, P], F32R, where=ph)
        route = sb("route", [P, EXPERTS + 1, 4], where=ph)
        rt = sb("rt", [P, 16, TILES, EXPERTS], where=ph)
        ecol = sb("ecol", [P, 4], where=ph)
        gcol = sb("gcol", [P, 4], where=ph)
        flag = sb("flag", [1, 1], I32, where=ph)
        ph.close()
        bank = ctx.enter_context(nc.psum_tensor("bank", [P, 8, 512], F32))

        ident = const[:, C_ID:C_ID + P]
        hid4 = hid[:, :, :].rearrange("p k (t n) -> p k t n", t=TILES)
        xhat = hid[:, :, :].rearrange("p k n -> p (k n)").rearrange("p (t d) -> p t d", t=TILES)
        stage = hid[:, :, :].rearrange("p k n -> p (k n)").rearrange("p (w t n) -> p w t n", w=2, t=TILES)
        gbT = gate[:, :, :].rearrange("p t d -> p (t d)")[:, 0:SCC * TILES * P].rearrange(
            "p (c t n) -> p c t n", c=SCC, t=TILES)
        heads_raw = work[:, 0:2 * HEADS * QK].rearrange("p (s h d) -> p s h d", s=2, h=HEADS)
        heads_sq = work[:, 2 * HEADS * QK:3 * HEADS * QK].rearrange("p (h d) -> p h d", h=HEADS)
        prow = work[:, 0:4 * P].rearrange("p (r n) -> p r n", r=4)
        prob_c = work[:, 0:HEADS * P].rearrange("p (h n) -> p h n", h=HEADS)
        prob_l = work[:, HEADS * P:].rearrange("p (h n) -> p h n", h=HEADS)
        rt2 = rt

        sems = {}

        def S(name):
            if name not in sems:
                sems[name] = ctx.enter_context(nc.semaphore(name))
            return sems[name]

        class Steps:

            def __init__(self, eng):
                self.eng, self.n = eng, {}

            def mark(self, ins, name):
                ins.then_inc(S(name), 1)
                self.n[name] = self.n.get(name, 0) + 1
                return self.n[name]

            def do(self, ins, name):
                self.eng.wait_ge(S(name), self.mark(ins, name))

        def cat(ap):
            return ap.rearrange("p a b -> p (a b)")

        def w_slot(ring, n, shape):
            size = 1
            for s in shape:
                size *= s
            v = ring[:, n, 0:size]
            if len(shape) == 2:
                return v.rearrange("p (a b) -> p a b", a=shape[0])
            if len(shape) == 3:
                return v.rearrange("p (a b c) -> p a b c", a=shape[0], b=shape[1])
            return v

        def width(piece):
            if piece[0] == "qb":
                return 2 * HEADS * QK
            if piece[0] == "kvb":
                return HEADS * (NOPE + VH)
            if piece[0] == "win" and piece[1] == 0:
                return KH * Z0
            return PIECE

        def gu_parts(w_gu, ff, u, kh):
            v = w_gu.rearrange("(h k p) n -> h p k n", p=P, k=KH)[kh]
            return v[:, :, u * UNIT:(u + 1) * UNIT], v[:, :, ff + u * UNIT:ff + (u + 1) * UNIT]

        def col_part(w, kh, c0, cw):
            return w.rearrange("(h k p) n -> h p k n", p=P, k=KH)[kh][:, :, c0:c0 + cw]

        def product(eng, *piece):
            eng.wait_ge(S("piece_used"), NUM[piece] + 1)

        block = ctx.enter_context(nc.Block())

        @block.sync
        def _(sp):
            def load(n, piece):
                slot, use = n % RAWS, n // RAWS
                arrived = S(f"raw_in{slot}")
                if n >= RAWS:
                    sp.wait_ge(S("low_ready"), n - RAWS + 1)
                kind = piece[0]
                if kind in ("ffn", "pw1") and piece[1] != "d":
                    w, ff = (t["ffn_gu"][0], D_FF) if kind == "ffn" else (t["conv_pw1"][0], D)
                    dst = w_slot(raw, slot, (KH, 2, UNIT))
                    g, u = gu_parts(w, ff, piece[2], "ab".index(piece[1]))
                    sp.dma_start(dst[:, :, 0, :], g).then_inc(arrived, 16)
                    sp.dma_start(dst[:, :, 1, :], u).then_inc(arrived, 16)
                    return 32
                if kind == "ffn":
                    dst = w_slot(raw, slot, (UC, D))
                    src = t["ffn_down"][0].rearrange("(u c p) n -> u p c n", p=P, c=UC)[piece[2]]
                elif kind == "ada":
                    (l, c), kh = piece[1], piece[2]
                    dst = w_slot(raw, slot, (KH, 512))
                    src = col_part(t["ada_w"][l], kh, c * 512, 512)
                elif kind == "win":
                    c0, cw = W_CHUNK[piece[1]]
                    dst = w_slot(raw, slot, (KH, cw))
                    src = col_part(t["w_in"][0], piece[2], c0, cw)
                elif kind == "qb":
                    dst = w_slot(raw, slot, (2, HEADS * QK))
                    src = t["w_qb"][0].rearrange("(k p) n -> p k n", p=P)
                elif kind == "kvb":
                    dst = w_slot(raw, slot, (1, D))
                    src = t["w_kvb"][0].rearrange("(k p) n -> p k n", p=P)
                else:
                    w = t["w_o"][0] if kind == "wo" else t["conv_pw2"][0]
                    dst = w_slot(raw, slot, (KH, 512))
                    src = col_part(w, piece[2], piece[1] * 512, 512)
                sp.dma_start(dst, src).then_inc(arrived, 16)
                return 16

            for n, piece in enumerate(ORDER):
                load(n, piece)

            def experts(first):
                with sp.Fori(0, EXPERTS) as e:
                    for i, (kind, u) in enumerate(STREAM_E):
                        slot = (first + i) % RAWS
                        arrived = S(f"raw_in{slot}")
                        sp.wait_ge(S("low_ready"), e * PER_E + (first + i - RAWS + 1))
                        if kind == "d":
                            src = t["moe_down"][0].rearrange("e (u c p) n -> e u p c n", p=P, c=UC)
                            sp.dma_start(w_slot(raw, slot, (UC, D)), src[bass.ds(e, 1), u]).then_inc(arrived, 16)
                        else:
                            kh = "ab".index(kind)
                            v = t["moe_gu"][0].rearrange("e (h k p) n -> e h p k n", p=P, k=KH)[bass.ds(e, 1), kh]
                            dst = w_slot(raw, slot, (KH, 2, UNIT))
                            c0 = u * UNIT
                            sp.dma_start(dst[:, :, 0, :], v[:, :, :, c0:c0 + UNIT]).then_inc(arrived, 16)
                            sp.dma_start(dst[:, :, 1, :],
                                         v[:, :, :, D_FFE + c0:D_FFE + c0 + UNIT]).then_inc(arrived, 16)

            experts(N_DENSE)
            sp.wait_ge(S("flag_ready"), 1)
            most = sp.value_load(flag[0:1, 0:1], min_val=0, max_val=TILES * P)
            with sp.If(most > P):
                experts(N_DENSE + EXPERTS * PER_E)
            sp.wait_ge(S("y_ready"), 1)
            sp.dma_start(outs[0][0], x[:, 0, :]).then_inc(S("y_out"), 16)
            sp.dma_start(outs[1][0], x[:, 1, :]).then_inc(S("y_out"), 16)
            sp.wait_ge(S("y_out"), 32)

        def loads_of(piece):
            return 2 if piece[0] in ("ffn", "pw1") and piece[1] != "d" else 1

        def arrived_value(n):
            return 16 * sum(loads_of(ORDER[m]) for m in range(n % RAWS, n + 1, RAWS))

        def slot_total(slot):
            return 16 * sum(loads_of(ORDER[m]) for m in range(slot, N_DENSE, RAWS))

        def expert_value(first, i):
            slot = (first + i) % RAWS
            within = sum(16 if STREAM_E[m][0] == "d" else 32 for m in range(i + 1) if (first + m) % RAWS == slot)
            per = sum(16 if STREAM_E[m][0] == "d" else 32 for m in range(PER_E) if (first + m) % RAWS == slot)
            passes = (first - N_DENSE) // (EXPERTS * PER_E)
            return slot_total(slot) + passes * EXPERTS * per + within, per

        @block.gpsimd
        def _(pool):
            st = Steps(pool)
            st.do(pool.memset(small[:, 48:64], -0.5), "exponent")

            def inverse_root(c0, cw, need):
                pool.wait_ge(S("ms_ready"), need)
                st.mark(pool.tensor_tensor(small[:, c0:c0 + cw], small[:, c0:c0 + cw], small[:, 48:48 + cw],
                                           ALU.pow), "rstd_ready")

            def gate_bias(i):
                l, c0 = i // 2, (2 if i % 2 == 0 else 5) * D
                src = t["ada_b"][l:l + 1, c0:c0 + D].partition_broadcast(P)
                if i == 0:
                    pool.wait_ge(S("sc_gated"), 1)
                else:
                    pool.wait_ge(S("residual"), i)
                for tt in range(TILES):
                    pool.dma_start(gate[:, tt, :], src).then_inc(S("gate_bias"), 16)

            inverse_root(0, 2, 1)
            inverse_root(0, 4, 2)
            pool.wait_ge(S("ckv_ready"), 2)
            pool.dma_start(outs[2][0, 0], kv_lat[:, 0, :]).then_inc(S("state_out"), 16)
            pool.dma_start(outs[3][0, 0], z0[:, 0, Q_LORA + KV_LORA:Z0]).then_inc(S("state_out"), 16)
            for i in range(5):
                inverse_root(0, HEADS, 3 + i)
            gate_bias(0)
            inverse_root(0, 2, 8)
            gate_bias(1)
            inverse_root(0, 2, 9)
            gate_bias(2)
            inverse_root(0, 2, 10)
            gate_bias(3)
            pool.wait_ge(S("state_out"), 32)

        @block.scalar
        def _(a):
            st = Steps(a)
            a.dma_start(const[:, :], t["table"]).then_inc(S("const_in"), 16)
            rows = {"c_ctx": t["c_ctx"].rearrange("(r f) -> r f", f=P),
                    "c": t["c"].rearrange("b (r f) -> (b r) f", f=P),
                    "norm_mix": t["norm_mix"].rearrange("l (r f) -> (l r) f", f=P),
                    "norm_ffn": t["norm_ffn"].rearrange("l (r f) -> (l r) f", f=P),
                    "pw1_b": t["conv_pw1_b"].rearrange("l (r f) -> (l r) f", f=P),
                    "dw_b": t["conv_dw_b"].rearrange("l (r f) -> (l r) f", f=P),
                    "ln_g": t["conv_ln_g"].rearrange("l (r f) -> (l r) f", f=P),
                    "ln_b": t["conv_ln_b"].rearrange("l (r f) -> (l r) f", f=P),
                    "w_sc": t["w_sc"][0].rearrange("j (r f) -> (j r) f", f=P),
                    "q_a": t["q_a_norm"].rearrange("l (r f) -> (l r) f", f=P)}
            for name, src in rows.items():
                a.dma_start(prow[ROWS[name]:ROWS[name] + src.shape[0], 0, :], src).then_inc(S("rows_in"), 16)
            a.dma_start(prow[0:96, 1, :], t["ada_b"].rearrange("l (r f) -> (l r) f", f=P)).then_inc(S("rows_in"), 16)
            for half in range(2):
                src = t["conv_dw"][0].rearrange("j (r f) -> (j r) f", f=P)[half * 124:(half + 1) * 124, :]
                a.dma_start(prow[0:124, 2 + half, :], src).then_inc(S("rows_in"), 16)
            a.dma_start(x[:, 0, :], t["x_prompt"][0]).then_inc(S("x_in"), 16)
            a.dma_start(x[:, 1, :], t["x_sample"][0]).then_inc(S("x_in"), 16)
            a.dma_start(kv_gain[:, :], t["kv_a_norm"].partition_broadcast(P)).then_inc(S("attn_in"), 16)
            a.dma_start(q_gain[:, :], t["q_norm"].partition_broadcast(P)).then_inc(S("attn_in"), 16)
            a.dma_start(k_gain[:, :], t["k_norm"].partition_broadcast(P)).then_inc(S("attn_in"), 16)
            a.dma_start(kv_lat[:, 2, :], t["cache_ckv"][0, 0]).then_inc(S("attn_in"), 16)
            a.dma_start(kpe_c[:, :], t["cache_kpe"][0, 0]).then_inc(S("attn_in"), 16)
            a.dma_start(router_w[:, :, :], t["router"][0].rearrange("(k p) n -> p k n", p=P)).then_inc(
                S("router_in"), 16)

            def high_part(n, w=PIECE):
                a.wait_ge(S(f"raw_in{n % RAWS}"), arrived_value(n))
                if n >= SPLITS:
                    a.wait_ge(S("piece_used"), n - SPLITS + 1)
                a.activation(high[:, n % SPLITS, 0:w], raw[:, n % RAWS, 0:w], ACT.Copy).then_inc(S("high_ready"), 1)

            def named(*piece):
                high_part(NUM[piece], width(piece))

            def ada(chunks):
                for c in chunks:
                    named("ada", c, 0)
                    named("ada", c, 1)

            def squares(i):
                if i:
                    a.wait_ge(S("residual"), i)
                else:
                    a.wait_ge(S("x_in"), 32)
                for tt in range(TILES):
                    st.mark(a.activation(xhat[:, tt, :], x[:, tt, :], ACT.Square,
                                         accum_out=small[:, 16 + tt:17 + tt]), "sum_sq")

            def hidden_high(names, need, k0=0, k1=KT):
                for tt in range(TILES):
                    a.wait_ge(S(names), need + tt)
                    st.mark(a.activation(hidH[:, k0:k1, tt * P:(tt + 1) * P], hid4[:, k0:k1, tt, :], ACT.Copy),
                            "hid_high")

            squares(0)
            a.wait_ge(S("rows_T"), 1)
            st.do(a.activation(cH[:, :, 0:2].rearrange("p k c -> p c k"),
                               bank[:, 7, 0:16].rearrange("p (c k) -> p c k", c=2), ACT.Silu), "silu_c")
            st.mark(a.activation(mod[:, 0, 0, :, :].rearrange("p k c -> p c k"),
                                 bank[:, 7, 0:16].rearrange("p (c k) -> p c k", c=2), ACT.Silu), "silu_c")
            ada(ADA_FIRST)
            named("win", 0, 0)
            hidden_high("hid_ready", 1)
            named("win", 0, 1)
            named("win", 2, 0)
            product(a, "win", 0, 1)
            for tt in range(TILES):
                st.mark(a.activation(z0[:, tt, :], bank[:, tt, 0:Z0], ACT.Copy), "z0_ready")
            named("win", 2, 1)
            product(a, "win", 2, 1)
            a.wait_ge(S("hid_low"), 2)
            for tt in range(TILES):
                st.mark(a.activation(stage[:, 0, tt, :], bank[:, 2 + tt, :], ACT.Copy), "gc_ready")
            named("qb")
            a.wait_ge(S("lat_T"), 1)
            for c in range(2):
                st.mark(a.activation(upH[:, 0, c, :].rearrange("p (t n) -> p t n", t=TILES),
                                     bank[:, 4, :].rearrange("p (t c n) -> p t c n", t=TILES, c=2)[:, :, c, :],
                                     ACT.Copy, scale=par[:, ROWS["q_a"] + c:ROWS["q_a"] + c + 1]), "lat_high")
            st.mark(a.activation(upH[:, 1, :, :].rearrange("p c n -> p (c n)")[:, 0:3 * P], bank[:, 5, 0:3 * P],
                                 ACT.Copy), "lat_high")
            named("kvb")
            named("win", 3, 0)

            def square_heads(i):
                a.wait_ge(S("heads_in"), i + 1)
                st.mark(a.activation(heads_sq, heads_raw[:, i % 2], ACT.Square), "heads_sq")

            def head_transposes_out(i):
                dst = qT[:, i] if i < 2 else kT[:, i - 2]
                a.wait_ge(S("heads_T"), i + 1)
                st.mark(a.activation(dst.rearrange("p h n -> p (h n)"), cat(bank[0:QK, 6:8, :]), ACT.Copy),
                        "heads_out")

            def values_out(i):
                b0 = (4, 0, 2)[i]
                a.wait_ge(S("heads_in"), 3 + i)
                src = cat(bank[:, b0:b0 + 2, :]).rearrange("p (h d) -> p h d", h=HEADS)[:, :, NOPE:]
                st.mark(a.activation(vals[:, i], src, ACT.Copy), "vals_ready")

            square_heads(0)
            square_heads(1)
            named("win", 3, 1)
            head_transposes_out(0)
            square_heads(2)
            values_out(0)
            named("win", 1, 0)
            head_transposes_out(1)
            square_heads(3)
            values_out(1)
            named("win", 1, 1)
            head_transposes_out(2)
            square_heads(4)
            values_out(2)
            product(a, "win", 1, 1)
            for tt in range(TILES):
                st.mark(a.activation(stage[:, 1, tt, :], bank[:, tt, :], ACT.Copy), "gb_ready")
            head_transposes_out(3)
            head_transposes_out(4)
            a.wait_ge(S("sc_T"), 1)
            for tt in range(TILES):
                st.mark(a.activation(gbT[:, :, tt, :], bank[:, 2 + tt, :].rearrange("p (c n) -> p c n", c=SCC),
                                     ACT.Copy), "gbT_ready")
            a.wait_ge(S("max_ready"), 1)
            for h in range(HEADS):
                st.mark(a.activation(prob_c[:, h, :], bank[:, h // 4, (h % 4) * P:(h % 4 + 1) * P], ACT.Exp,
                                     bias=small[:, 24 + h:25 + h], scale=SCALE,
                                     accum_out=small[:, 8 + h:9 + h]), "exp_c")
            a.wait_ge(S("max_ready"), 2)
            for h in range(HEADS):
                st.mark(a.activation(prob_l[:, h, :], bank[:, 2 + h // 2, (h % 2) * 256:(h % 2 + 1) * 256], ACT.Exp,
                                     bias=small[:, 32 + h:33 + h],
                                     scale=SCALE, accum_out=small[:, 16 + h:17 + h]), "exp_l")
            for g in range(6):
                a.wait_ge(S("prob_T"), g + 1)
                if g >= 2:
                    a.wait_ge(S("pv_group"), g - 1)
                st.mark(a.activation(cat(probT[:, g % 2]), bank[:, g % 2, :], ACT.Copy), "probT_ready")
            ada(ADA_ATTN)
            ada(ADA_GATE[0])
            for tt in range(TILES):
                a.wait_ge(S("pv_group"), 2 if tt == 0 else 6)
                st.mark(a.activation(hidH[:, 0:4, tt * P:(tt + 1) * P],
                                     bank[:, 2 + tt, :].rearrange("p (c n) -> p c n", c=4), ACT.Copy), "hid_high")
            a.wait_ge(S("sc_gated"), 1)
            for tt in range(TILES):
                st.mark(a.activation(hidH[:, 4:8, tt * P:(tt + 1) * P], hid4[:, 4:8, tt, :], ACT.Copy), "hid_high")
            for h in (0, 1):
                named("wo", h, 0)
                named("wo", h, 1)
            squares(1)
            ada(ADA_GATE[1])
            hidden_high("hid_ready", 3)

            def unit_high(kind, u):
                named("ffn", kind, u)

            n_units = D_FF // UNIT
            unit_high("a", 0)
            unit_high("b", 0)
            for u in range(n_units):
                if u + 1 < n_units:
                    unit_high("a", u + 1)
                product(a, "ffn", "b", u)
                if u >= 2:
                    a.wait_ge(S("ffn_T"), u - 1)
                for tt in range(TILES):
                    st.mark(a.activation(act[:, u % 2, tt, :], bank[:, tt, 0:UNIT], ACT.Silu), "ffn_silu")
                if u + 1 < n_units:
                    unit_high("b", u + 1)
                for v in ([u - 1] if u >= 1 else []) + ([u] if u + 1 == n_units else []):
                    a.wait_ge(S("ffn_T"), v + 1)
                    if v >= 2:
                        a.wait_ge(S("piece_used"), NUM[("ffn", "d", v - 2)] + 1)
                    src = bank[:, 6, :].rearrange("p (t c n) -> p c t n", t=TILES, c=UC)
                    st.mark(a.activation(upH[:, v % 2].rearrange("p c (t n) -> p c t n", t=TILES), src, ACT.Copy),
                            "ffn_high")
                    unit_high("d", v)
            squares(2)
            a.dma_start(pw2_b[:, :], t["conv_pw2_b"]).then_inc(S("pw2_bias_in"), 16)
            ada(ADA_GATE[2])
            hidden_high("hid_ready", 5)
            for u in range(4):
                named("pw1", "a", u)
                named("pw1", "b", u)
                product(a, "pw1", "b", u)
                if u >= 2:
                    a.wait_ge(S("pw1_T"), u - 1)
                b0 = 2 * (u % 2)
                for tt in range(TILES):
                    st.mark(a.activation(ag[:, u % 2, tt, :], bank[:, b0 + tt, :], ACT.Copy), "ag_ready")
                a.wait_ge(S("pw1_T"), u + 1)
                if u:
                    a.wait_ge(S("glu_ready"), UC * u)
                for c in range(UC):
                    k = u * UC + c
                    src = bank[:, 4:6, (UC + c) * P:(UC + c + 1) * P]
                    st.mark(a.activation(sg[:, c], src, ACT.Sigmoid,
                                         bias=par[:, ROWS["pw1_b"] + KT + k:ROWS["pw1_b"] + KT + k + 1]),
                            "sg_ready")
            a.wait_ge(S("centred"), 1)
            st.mark(a.activation(sq[:, :, :], hid[:, :, :], ACT.Square), "sq_ready")
            a.wait_ge(S("inv_var"), 1)
            st.mark(a.activation(stat[:, 1, :], stat[:, 0, :], ACT.Sqrt), "ln_rstd")
            for k in range(KT):
                a.wait_ge(S("ln_scaled"), 1)
                st.do(a.activation(hid[:, k, :], hid[:, k, :], ACT.Silu,
                                   bias=par[:, ROWS["ln_b"] + k:ROWS["ln_b"] + k + 1],
                                   scale=par[:, ROWS["ln_g"] + k:ROWS["ln_g"] + k + 1]), "ln_silu")
            for tt in range(TILES):
                st.mark(a.activation(hidH[:, :, tt * P:(tt + 1) * P], hid4[:, :, tt, :], ACT.Copy), "hid_high")
            for h in (0, 1):
                named("pw2", h, 0)
                named("pw2", h, 1)
            squares(3)
            ada(ADA_GATE[3])
            for tt in range(TILES):
                a.wait_ge(S("tok_T"), tt + 1)
                st.mark(a.activation(tokH[:, tt, :], cat(bank[:, 2 * tt:2 * tt + 2, :]), ACT.Copy), "tok_high")
            a.wait_ge(S("top2_diff"), 1)
            st.mark(a.activation(small[:, 2:4], small[:, 0:2], ACT.Exp), "top2_exp")

            def gather_out(base):
                for part, dst in enumerate((slotH, slotL)):
                    for kh in range(2):
                        i = 2 * part + kh
                        a.wait_ge(S("gathered"), base + i + 1)
                        a.activation(cat(dst[:, kh * KH:(kh + 1) * KH, :]), bank[:, 6 + kh, :],
                                     ACT.Copy).then_inc(S("slot_ready"), 1)

            def experts(first, passes):
                a.wait_ge(S("pick_ready"), 1 + passes * (EXPERTS + 1))
                a.activation(pickR[:, :, :], pick[:, :, :], ACT.Copy).then_inc(S("pickR_ready"), 1)
                gather_out(passes * 4 * (EXPERTS + 1))
                with a.Fori(0, EXPERTS) as e:
                    ge = passes * EXPERTS

                    def part(kind, u):
                        i = NUM_E[(kind, u)]
                        n = first + i
                        v, per = expert_value(first, i)
                        a.wait_ge(S(f"raw_in{n % RAWS}"), e * per + v)
                        a.wait_ge(S("piece_used"), e * PER_E + (n - SPLITS + 1))
                        a.activation(high[:, n % SPLITS, :], raw[:, n % RAWS, :], ACT.Copy).then_inc(
                            S("high_ready"), 1)

                    def act_high(v):
                        a.wait_ge(S("e_T"), e * UNITS_E + (ge * UNITS_E + v + 1))
                        if v >= 2:
                            a.wait_ge(S("piece_used"), e * PER_E + (first + NUM_E[("d", v - 2)] + 1))
                        a.activation(upH[:, v % 2, :, 0:P], bank[:, 2 + v % 2, 0:UNIT].rearrange(
                            "p (c n) -> p c n", c=UC), ACT.Copy).then_inc(S("e_high"), 1)

                    part("a", 0)
                    part("b", 0)
                    for u in range(UNITS_E):
                        if u + 1 < UNITS_E:
                            part("a", u + 1)
                        a.wait_ge(S("piece_used"), e * PER_E + (first + NUM_E[("b", u)] + 1))
                        a.activation(eact[:, u % 2, :], bank[:, u % 2, 0:UNIT], ACT.Silu).then_inc(S("e_silu"), 1)
                        if u == 0:
                            a.wait_ge(S("back_T"), e + (ge + 1))
                            a.activation(cat(backR[:, :, :]), bank[:, 6, 0:TILES * P], ACT.Copy).then_inc(
                                S("back_ready"), 1)
                        if u + 1 < UNITS_E:
                            part("b", u + 1)
                        if u >= 1:
                            act_high(u - 1)
                            part("d", u - 1)
                    a.wait_ge(S("pick_ready"), e + (2 + passes * (EXPERTS + 1)))
                    a.activation(pickR[:, :, :], pick[:, :, :], ACT.Copy).then_inc(S("pickR_ready"), 1)
                    gather_out(e * 4 + (4 + passes * 4 * (EXPERTS + 1)))
                    act_high(UNITS_E - 1)
                    part("d", UNITS_E - 1)
                    for h in range(2):
                        a.wait_ge(S("piece_used"), e * PER_E + (first + PER_E))
                        a.activation(outH[:, h * 512:(h + 1) * 512], bank[:, 4 + h, :], ACT.Copy).then_inc(
                            S("out_high"), 1)

            experts(N_DENSE, 0)
            a.wait_ge(S("flag_ready"), 1)
            most = a.value_load(flag[0:1, 0:1], min_val=0, max_val=TILES * P)
            with a.If(most > P):
                experts(N_DENSE + EXPERTS * PER_E, 1)

        @block.vector
        def _(v):
            st = Steps(v)

            def low_part(n, w=PIECE):
                v.wait_ge(S("high_ready"), n + 1)
                v.tensor_tensor(low[:, n % SPLITS, 0:w], raw[:, n % RAWS, 0:w],
                                high[:, n % SPLITS, 0:w].bitcast(F32), ALU.subtract).then_inc(S("low_ready"), 1)

            def named(*piece):
                low_part(NUM[piece], width(piece))

            def rms_scale(i, ms_count):
                v.wait_ge(S("sum_sq"), 2 * i + 2)
                st.do(v.tensor_scalar(small[:, 0:2], small[:, 16:18], 1.0 / D, EPS, ALU.mult, ALU.add), "ms_ready")
                v.wait_ge(S("rstd_ready"), ms_count)
                for tt in range(TILES):
                    st.mark(v.tensor_scalar(xhat[:, tt, :], x[:, tt, :], small[:, tt:tt + 1], None, ALU.mult),
                            "xhat_ready")

            def gain_scale(i):
                l, w = i // 2, i % 2
                g0 = ROWS["norm_ffn" if w else "norm_mix"] + l * KT
                g = par[:, g0:g0 + KT].unsqueeze(2).to_broadcast([P, KT, 2])
                st.do(v.scalar_tensor_tensor(aff[:, :, :], mod[:, l, 2 * w + 1], 1.0, g, ALU.add, ALU.mult),
                      "aff_ready")

            def modulate(i):
                l, w = i // 2, i % 2
                v.wait_ge(S("xhat_T"), i + 1)
                for tt in range(TILES):
                    for k in range(KT):
                        ins = v.tensor_scalar(hid4[:, k, tt, :],
                                              bank[:, 2 * tt + k // 4, (k % 4) * P:(k % 4 + 1) * P],
                                              aff[:, k, tt:tt + 1], mod[:, l, 2 * w, k, tt:tt + 1],
                                              ALU.mult, ALU.add)
                        if k == KT - 1:
                            st.do(ins, "hid_ready")
                        else:
                            st.mark(ins, "hid_parts")

            def hidden_low(high_count):
                for tt in range(TILES):
                    v.wait_ge(S("hid_high"), high_count + tt + 1)
                    st.mark(v.tensor_tensor(hidL[:, :, tt * P:(tt + 1) * P], hid4[:, :, tt, :],
                                            hidH[:, :, tt * P:(tt + 1) * P].bitcast(F32), ALU.subtract), "hid_low")

            ada_n = [0]
            gate_n = [0]

            def ada_out(l, c):
                ada_n[0] += 1
                product(v, "ada", (l, c), 1)
                if ada_n[0] > 1:
                    v.wait_ge(S("ada_summed"), ada_n[0] - 1)
                st.mark(v.tensor_copy(ada4[:, :], bank[0:4, 6, :]), "ada4_ready")
                v.wait_ge(S("ada_summed"), ada_n[0])
                part, half = c // 2, c % 2
                if part in (2, 5):
                    gate_n[0] += 1
                    v.wait_ge(S("gate_bias"), 32 * ((gate_n[0] + 1) // 2))
                    for tt in range(TILES):
                        b = 7 if tt == 0 else 6
                        dst = gate[:, tt, half * 512:(half + 1) * 512]
                        st.do(v.tensor_tensor(dst, bank[:, b, :], dst, ALU.add), "ada_out")
                else:
                    m = {0: 0, 1: 1, 3: 2, 4: 3}[part]
                    dst = mod[:, l, m, half * 4:half * 4 + 4, :]
                    bias = ada_bT[:, l * 48 + c * 4:l * 48 + c * 4 + 4].unsqueeze(2).to_broadcast([P, 4, 2])
                    st.do(v.tensor_tensor(dst, bank[:, 7, 0:8].rearrange("p (k c) -> p k c", c=2), bias, ALU.add),
                          "ada_out")

            def ada(chunks):
                for l, c in chunks:
                    named("ada", (l, c), 0)
                    named("ada", (l, c), 1)
                    ada_out(l, c)

            def residual():
                for tt in range(TILES):
                    for h in range(2):
                        tmp = stage[:, tt, h, :]
                        st.do(v.tensor_tensor(tmp, bank[:, 2 + 2 * tt + h, :],
                                              gate[:, tt, h * 512:(h + 1) * 512], ALU.mult), "res_part")
                        xs = x[:, tt, h * 512:(h + 1) * 512]
                        ins = v.tensor_tensor(xs, xs, tmp, ALU.add)
                        if tt == 1 and h == 1:
                            st.do(ins, "residual")
                        else:
                            st.do(ins, "res_part")

            rms_scale(0, 1)
            v.wait_ge(S("silu_c"), 2)
            st.do(v.tensor_copy(par[:, :], bank[:, 7, 0:NROWS]), "rows_out")
            st.do(v.tensor_copy(ada_bT[:, :], bank[:, 6, 0:96]), "rows_out")
            st.do(v.tensor_copy(taps[:, :], bank[:, 6, 96:96 + 248]), "rows_out")
            st.do(v.tensor_tensor(cH[:, :, 2:4], mod[:, 0, 0, :, :], cH[:, :, 0:2].bitcast(F32), ALU.subtract),
                  "c_low")
            ada(ADA_FIRST)
            gain_scale(0)
            modulate(0)
            named("win", 0, 0)
            hidden_low(0)
            named("win", 0, 1)
            named("win", 2, 0)
            v.wait_ge(S("z0_ready"), 2)
            for tt in range(TILES):
                q = z0[:, tt, 0:Q_LORA]
                k = z0[:, tt, Q_LORA:Q_LORA + KV_LORA]
                st.do(v.tensor_tensor(work[:, 0:Q_LORA], q, q, ALU.mult), "lat_part")
                st.do(v.tensor_reduce(small[:, 8 + tt:9 + tt], work[:, 0:Q_LORA], AX, ALU.add), "lat_part")
                st.do(v.tensor_tensor(work[:, 0:KV_LORA], k, k, ALU.mult), "lat_part")
                st.do(v.tensor_reduce(small[:, 10 + tt:11 + tt], work[:, 0:KV_LORA], AX, ALU.add), "lat_part")
            st.do(v.tensor_scalar(small[:, 0:2], small[:, 8:10], 1.0 / Q_LORA, EPS, ALU.mult, ALU.add), "lat_part")
            st.do(v.tensor_scalar(small[:, 2:4], small[:, 10:12], 1.0 / KV_LORA, EPS, ALU.mult, ALU.add), "ms_ready")
            v.wait_ge(S("rstd_ready"), 2)
            v.wait_ge(S("attn_in"), 80)
            for tt in range(TILES):
                st.do(v.scalar_tensor_tensor(kv_lat[:, tt, :], z0[:, tt, Q_LORA:Q_LORA + KV_LORA],
                                             small[:, 2 + tt:3 + tt], kv_gain[:, :], ALU.mult, ALU.mult),
                      "ckv_ready")
            for tt in range(TILES):
                q = z0[:, tt, 0:Q_LORA]
                st.do(v.tensor_scalar(q, q, small[:, tt:tt + 1], None, ALU.mult), "qlat_ready")
            named("win", 2, 1)
            named("qb")
            v.wait_ge(S("lat_high"), 3)
            for c in range(2):
                st.mark(v.scalar_tensor_tensor(
                    upL[:, 0, c, :].rearrange("p (t n) -> p t n", t=TILES),
                    bank[:, 4, :].rearrange("p (t c n) -> p t c n", t=TILES, c=2)[:, :, c, :],
                    par[:, ROWS["q_a"] + c:ROWS["q_a"] + c + 1],
                    upH[:, 0, c, :].rearrange("p (t n) -> p t n", t=TILES).bitcast(F32),
                    ALU.mult, ALU.subtract), "lat_low")
            st.mark(v.tensor_tensor(upL[:, 1, :, :].rearrange("p c n -> p (c n)")[:, 0:3 * P], bank[:, 5, 0:3 * P],
                                    upH[:, 1, :, :].rearrange("p c n -> p (c n)")[:, 0:3 * P].bitcast(F32),
                                    ALU.subtract), "lat_low")
            named("kvb")
            named("win", 3, 0)

            def heads_in(i):
                dst = heads_raw[:, i % 2]
                if i >= 2:
                    v.wait_ge(S("heads_T"), i - 1)
                if i < 2:
                    if i == 0:
                        v.wait_ge(S("q_product"), 1)
                    else:
                        product(v, "qb")
                    src = bank[:, 2 * i:2 * i + 2, 0:4 * QK]
                    st.do(v.tensor_copy(dst.rearrange("p (a h) d -> p a (h d)", a=2), src), "heads_in")
                else:
                    j = i - 2
                    b0 = (4, 0, 2)[j]
                    if j < 2:
                        v.wait_ge(S("kv_product"), j + 1)
                    else:
                        product(v, "kvb")
                    src = cat(bank[:, b0:b0 + 2, :]).rearrange("p (h d) -> p h d", h=HEADS)[:, :, 0:NOPE]
                    st.do(v.tensor_copy(dst[:, :, 0:NOPE], src), "nope_in")
                    kpe = z0[:, j, Q_LORA + KV_LORA:Z0] if j < 2 else kpe_c[:, :]
                    st.do(v.tensor_copy(dst[:, :, NOPE:], kpe.unsqueeze(1).to_broadcast([P, HEADS, ROPE])),
                          "heads_in")

            def heads_norm(i):
                h = heads_raw[:, i % 2]
                v.wait_ge(S("heads_sq"), i + 1)
                st.do(v.tensor_reduce(small[:, 8:16], heads_sq, AX, ALU.add), "heads_part")
                st.do(v.tensor_scalar(small[:, 0:8], small[:, 8:16], 1.0 / QK, EPS, ALU.mult, ALU.add), "ms_ready")
                v.wait_ge(S("rstd_ready"), 3 + i)
                st.do(v.tensor_tensor(h, h, small[:, 0:8].unsqueeze(2).to_broadcast([P, HEADS, QK]), ALU.mult),
                      "heads_part")
                g = (q_gain if i < 2 else k_gain)[:, :].unsqueeze(1).to_broadcast([P, HEADS, QK])
                rotate = i in (1, 3)
                st.do(v.tensor_tensor(h, h, g, ALU.mult), "heads_part" if rotate else "heads_normed")
                if rotate:
                    half = ROPE // 4
                    cos = const[:, C_COS:C_SIN].rearrange("p (h d) -> p h d", h=HEADS)
                    sin = const[:, C_SIN:C_SUM2].rearrange("p (h d) -> p h d", h=HEADS)
                    for axis in range(2):
                        for s in range(2):
                            d0 = (2 * axis + s) * half
                            o0 = (2 * axis + 1 - s) * half
                            st.do(v.tensor_tensor(rope_t[:, :, d0:d0 + half],
                                                  h[:, :, NOPE + o0:NOPE + o0 + half],
                                                  sin[:, :, d0:d0 + half], ALU.mult), "heads_part")
                    st.do(v.tensor_tensor(h[:, :, NOPE:], h[:, :, NOPE:], cos, ALU.mult), "heads_part")
                    st.do(v.tensor_tensor(h[:, :, NOPE:], h[:, :, NOPE:], rope_t[:, :, :], ALU.add), "heads_normed")

            v.wait_ge(S("const_in"), 16)
            heads_in(0)
            heads_norm(0)
            heads_in(1)
            named("win", 3, 1)
            heads_norm(1)
            heads_in(2)
            named("win", 1, 0)
            heads_norm(2)
            heads_in(3)
            named("win", 1, 1)
            heads_norm(3)
            heads_in(4)
            v.wait_ge(S("gc_ready"), 2)
            product(v, "win", 3, 1)
            for tt in range(TILES):
                st.do(v.tensor_tensor(stage[:, 0, tt, :], stage[:, 0, tt, :], bank[:, 4 + tt, :], ALU.mult),
                      "v_ready")
            heads_norm(4)
            st.do(v.memset(vTpad[:, :, :, 0:1], 0.0), "pads")
            st.do(v.memset(vTpad[:, :, :, P + 1:P + 2], 0.0), "pads")
            v.wait_ge(S("sc_T"), 1)
            for tt in range(TILES):
                st.do(v.tensor_copy(vTpad[:, :, tt, 1:P + 1],
                                    bank[:, tt, :].rearrange("p (c n) -> p c n", c=SCC)), "vT_ready")
            v.wait_ge(S("scores"), 1)
            st.do(v.tensor_reduce(small[:, 24:32], cat(bank[:, 0:2, :]).rearrange("p (h n) -> p h n", h=HEADS),
                                  AX, ALU.max), "max_part")
            st.do(v.tensor_scalar(small[:, 24:32], small[:, 24:32], -SCALE, None, ALU.mult), "max_ready")
            v.wait_ge(S("scores"), 2)
            st.do(v.tensor_reduce(small[:, 32:40], cat(bank[:, 2:6, :]).rearrange("p (h n) -> p h n", h=HEADS),
                                  AX, ALU.max), "max_part")
            st.do(v.tensor_scalar(small[:, 32:40], small[:, 32:40], -SCALE, None, ALU.mult), "max_ready")
            v.wait_ge(S("exp_c"), HEADS)
            st.do(v.reciprocal(small[:, 0:8], small[:, 8:16]), "max_part")
            st.do(v.tensor_tensor(prob_c, prob_c, small[:, 0:8].unsqueeze(2).to_broadcast([P, HEADS, P]), ALU.mult),
                  "prob_ready")
            v.wait_ge(S("exp_l"), HEADS)
            st.do(v.reciprocal(small[:, 0:8], small[:, 16:24]), "max_part")
            st.do(v.tensor_tensor(prob_l, prob_l, small[:, 0:8].unsqueeze(2).to_broadcast([P, HEADS, 2 * P]),
                                  ALU.mult), "prob_ready")
            v.wait_ge(S("gbT_ready"), 2)
            for c in range(SCC):
                for j in range(3):
                    w = par[:, ROWS["w_sc"] + j * SCC + c:ROWS["w_sc"] + j * SCC + c + 1]
                    src = vTpad[:, c, :, j:j + P]
                    dst = hid4[:, 4 + c, :, :]
                    if j == 0:
                        st.do(v.tensor_scalar(dst, src, w, None, ALU.mult), "sc_part")
                    else:
                        st.do(v.scalar_tensor_tensor(dst, src, w, dst, ALU.mult, ALU.add), "sc_part")
            st.do(v.tensor_tensor(hid[:, 4:8, :].rearrange("p k n -> p (k n)"),
                                  hid[:, 4:8, :].rearrange("p k n -> p (k n)"),
                                  gbT.rearrange("p c t n -> p (c t n)"), ALU.mult), "sc_gated")
            ada(ADA_ATTN)
            ada(ADA_GATE[0])
            for tt in range(TILES):
                v.wait_ge(S("hid_high"), 2 + tt + 1)
                st.mark(v.tensor_tensor(hidL[:, 0:4, tt * P:(tt + 1) * P],
                                        bank[:, 2 + tt, :].rearrange("p (c n) -> p c n", c=4),
                                        hidH[:, 0:4, tt * P:(tt + 1) * P].bitcast(F32), ALU.subtract), "hid_low")
            for tt in range(TILES):
                v.wait_ge(S("hid_high"), 4 + tt + 1)
                st.mark(v.tensor_tensor(hidL[:, 4:8, tt * P:(tt + 1) * P], hid4[:, 4:8, tt, :],
                                        hidH[:, 4:8, tt * P:(tt + 1) * P].bitcast(F32), ALU.subtract), "hid_low")
            for h in (0, 1):
                named("wo", h, 0)
                named("wo", h, 1)
            product(v, "wo", 1, 1)
            v.wait_ge(S("hid_low"), 6)
            residual()
            rms_scale(1, 8)
            gain_scale(1)
            ada(ADA_GATE[1])
            modulate(1)
            hidden_low(6)
            n_units = D_FF // UNIT
            named("ffn", "a", 0)
            named("ffn", "b", 0)
            for u in range(n_units):
                if u + 1 < n_units:
                    named("ffn", "a", u + 1)
                for tt in range(TILES):
                    v.wait_ge(S("ffn_silu"), TILES * u + tt + 1)
                    at = act[:, u % 2, tt, :]
                    st.mark(v.tensor_tensor(at, at, bank[:, tt, UNIT:2 * UNIT], ALU.mult), "ffn_act")
                if u + 1 < n_units:
                    named("ffn", "b", u + 1)
                for w in ([u - 1] if u >= 1 else []) + ([u] if u + 1 == n_units else []):
                    v.wait_ge(S("ffn_high"), w + 1)
                    src = bank[:, 6, :].rearrange("p (t c n) -> p c t n", t=TILES, c=UC)
                    for c in range(UC):
                        st.mark(v.tensor_tensor(upL[:, w % 2, c, :].rearrange("p (t n) -> p t n", t=TILES),
                                                src[:, c],
                                                upH[:, w % 2, c, :].rearrange("p (t n) -> p t n", t=TILES).bitcast(F32),
                                                ALU.subtract), "ffn_low")
                    named("ffn", "d", w)
            product(v, "ffn", "d", n_units - 1)
            residual()
            rms_scale(2, 9)
            gain_scale(2)
            ada(ADA_GATE[2])
            modulate(2)
            hidden_low(8)
            st.do(v.memset(uT[:, :, :, 0:PAD], 0.0), "pads")
            st.do(v.memset(uT[:, :, :, PAD + P:], 0.0), "pads")
            for u in range(4):
                named("pw1", "a", u)
                named("pw1", "b", u)
                for c in range(UC):
                    k = u * UC + c
                    v.wait_ge(S("sg_ready"), UC * (u + 1))
                    b = par[:, ROWS["pw1_b"] + k:ROWS["pw1_b"] + k + 1]
                    st.do(v.scalar_tensor_tensor(uT[:, k, :, PAD:PAD + P], bank[:, 4:6, c * P:(c + 1) * P], b,
                                                 sg[:, c], ALU.add, ALU.mult), "glu_ready")
            v.wait_ge(S("hid_low"), 10)
            for k in range(KT):
                dst = hid4[:, k, :, :]
                for j in range(TAPS):
                    w = taps[:, j * KT + k:j * KT + k + 1]
                    src = uT[:, k, :, j:j + P]
                    if j == 0:
                        b = par[:, ROWS["dw_b"] + k:ROWS["dw_b"] + k + 1]
                        st.do(v.tensor_scalar(dst, src, w, b, ALU.mult, ALU.add), "conv_part")
                    else:
                        st.do(v.scalar_tensor_tensor(dst, src, w, dst, ALU.mult, ALU.add),
                              "conv_ready" if j == TAPS - 1 else "conv_part")
            v.wait_ge(S("ln_sum"), 1)
            st.do(v.tensor_scalar(stat[:, 0, :], bank[:, 0, 0:TILES * P], 1.0 / D, None, ALU.mult), "ln_part")
            st.do(v.tensor_tensor(hid[:, :, :], hid[:, :, :],
                                  stat[:, 0, :].unsqueeze(1).to_broadcast([P, KT, TILES * P]), ALU.subtract),
                  "centred")
            v.wait_ge(S("ln_sum"), 2)
            st.do(v.tensor_scalar(stat[:, 0, :], bank[:, 1, 0:TILES * P], 1.0 / D, EPS, ALU.mult, ALU.add), "ln_part")
            st.do(v.reciprocal(stat[:, 0, :], stat[:, 0, :]), "inv_var")
            v.wait_ge(S("ln_rstd"), 1)
            st.do(v.tensor_tensor(hid[:, :, :], hid[:, :, :],
                                  stat[:, 1, :].unsqueeze(1).to_broadcast([P, KT, TILES * P]), ALU.mult),
                  "ln_scaled")
            v.wait_ge(S("ln_silu"), KT)
            hidden_low(10)
            for h in (0, 1):
                named("pw2", h, 0)
                named("pw2", h, 1)
            product(v, "pw2", 1, 1)
            v.wait_ge(S("hid_low"), 12)
            residual()
            rms_scale(3, 10)
            gain_scale(3)
            ada(ADA_GATE[3])
            modulate(3)

            LG, M1, EQ, MASK1, LG2, MASK2, G, M, TMP, POS = range(10)
            r = lambda i: rt[:, i]
            iota8 = const[:, C_IOTA:C_IOTA + EXPERTS].unsqueeze(1).to_broadcast([P, TILES, EXPERTS])

            def wide(c0):
                return small[:, c0:c0 + TILES].unsqueeze(2).to_broadcast([P, TILES, EXPERTS])

            def first_of_max(logits, c_max, c_idx, out):
                st.do(v.tensor_reduce(small[:, c_max:c_max + TILES], r(logits), AX, ALU.max), "route_part")
                st.do(v.tensor_tensor(r(EQ), r(logits), wide(c_max), ALU.is_equal), "route_part")
                st.do(v.scalar_tensor_tensor(r(EQ), r(EQ), -float(EXPERTS), iota8, ALU.mult, ALU.add), "route_part")
                st.do(v.tensor_reduce(small[:, c_idx:c_idx + TILES], r(EQ), AX, ALU.min), "route_part")
                st.do(v.tensor_scalar(small[:, c_idx:c_idx + TILES], small[:, c_idx:c_idx + TILES],
                                      float(EXPERTS), None, ALU.add), "route_part")
                st.do(v.tensor_tensor(r(out), iota8, wide(c_idx), ALU.is_equal), "route_part")

            v.wait_ge(S("logits"), 1)
            st.do(v.tensor_copy(r(LG), bank[:, 4, 0:TILES * EXPERTS].rearrange("p (t e) -> p t e", t=TILES)),
                  "route_part")
            first_of_max(LG, 8, 12, MASK1)
            st.do(v.scalar_tensor_tensor(r(LG2), r(MASK1), -3.0e38, r(LG), ALU.mult, ALU.add), "route_part")
            first_of_max(LG2, 10, 12, MASK2)
            st.do(v.tensor_tensor(small[:, 0:2], small[:, 10:12], small[:, 8:10], ALU.subtract), "top2_diff")
            st.do(v.tensor_tensor(r(M), r(MASK1), r(MASK2), ALU.add), "chosen")
            v.wait_ge(S("top2_exp"), 1)
            st.do(v.tensor_scalar(small[:, 4:6], small[:, 2:4], 1.0, None, ALU.add), "route_part")
            st.do(v.reciprocal(small[:, 4:6], small[:, 4:6]), "route_part")
            st.do(v.tensor_tensor(small[:, 6:8], small[:, 2:4], small[:, 4:6], ALU.mult), "route_part")
            st.do(v.tensor_tensor(r(MASK1), r(MASK1), wide(4), ALU.mult), "route_part")
            st.do(v.tensor_tensor(r(MASK2), r(MASK2), wide(6), ALU.mult), "route_part")
            st.do(v.tensor_tensor(r(G), r(MASK1), r(MASK2), ALU.add), "route_part")
            st.do(v.memset(route[:, :, :], -1.0), "route_part")
            st.do(v.tensor_copy(route[:, 0:EXPERTS, 2:4].rearrange("p e t -> p t e"), r(G)), "route_part")
            v.wait_ge(S("slots"), 1)
            pos = bank[:, 5, 0:TILES * EXPERTS].rearrange("p (t e) -> p t e", t=TILES)
            st.do(v.scalar_tensor_tensor(r(POS), pos, 1.0, r(M), ALU.add, ALU.mult), "route_part")
            st.do(v.tensor_scalar(route[:, 0:EXPERTS, 0:2].rearrange("p e t -> p t e"), r(POS), -1.0, None, ALU.add),
                  "route_part")
            st.do(v.tensor_reduce(small[:, 14:15], bank[:, 5, 16:16 + EXPERTS], AX, ALU.max), "route_part")
            st.do(v.tensor_copy(flag[0:1, 0:1], small[0:1, 14:15]), "flag_ready")
            for tt in range(TILES):
                v.wait_ge(S("tok_high"), tt + 1)
                st.mark(v.tensor_tensor(tokL[:, tt, :], cat(bank[:, 2 * tt:2 * tt + 2, :]),
                                        tokH[:, tt, :].bitcast(F32), ALU.subtract), "tok_low")
            v.wait_ge(S("tok_T"), TILES)
            v.wait_ge(S("logits"), 1)
            st.do(v.memset(xhat[:, :, :], 0.0), "y_part")

            def experts(first, passes):
                pe0 = passes * (EXPERTS + 1)
                ge = passes * EXPERTS

                def pick_of(e, count, done):
                    v.tensor_copy(ecol[:, :], route[:, bass.ds(e, 1), :].rearrange("p a b -> p (a b)")
                                  ).then_inc(S("ecol_ready"), 1)
                    v.wait_ge(S("ecol_ready"), count(1))
                    v.tensor_scalar(ecol[:, 0:2], ecol[:, 0:2], -float(passes * P), None, ALU.add).then_inc(
                        S("ecol_ready"), 1)
                    v.wait_ge(S("ecol_ready"), count(2))
                    v.tensor_scalar(pick[:, 0, :], const[:, C_IOTA:C_IOTA + P], ecol[:, 0:1], None,
                                    ALU.is_equal).then_inc(S("ecol_ready"), 1)
                    v.tensor_scalar(pick[:, 1, :], const[:, C_IOTA:C_IOTA + P], ecol[:, 1:2], None,
                                    ALU.is_equal).then_inc(S("pick_ready"), 1)
                    v.wait_ge(S("pick_ready"), done)

                pick_of(0, lambda m: 3 * pe0 + m, pe0 + 1)
                with v.Fori(0, EXPERTS) as e:
                    def part(kind, u):
                        i = NUM_E[(kind, u)]
                        n = first + i
                        v.wait_ge(S("high_ready"), e * PER_E + (n + 1))
                        v.tensor_tensor(low[:, n % SPLITS, :], raw[:, n % RAWS, :],
                                        high[:, n % SPLITS, :].bitcast(F32), ALU.subtract).then_inc(
                                            S("low_ready"), 1)

                    def act_low(w):
                        v.wait_ge(S("e_high"), e * UNITS_E + (ge * UNITS_E + w + 1))
                        v.tensor_tensor(upL[:, w % 2, :, 0:P],
                                        bank[:, 2 + w % 2, 0:UNIT].rearrange("p (c n) -> p c n", c=UC),
                                        upH[:, w % 2, :, 0:P].bitcast(F32), ALU.subtract).then_inc(S("e_low"), 1)

                    part("a", 0)
                    part("b", 0)
                    for u in range(UNITS_E):
                        if u + 1 < UNITS_E:
                            part("a", u + 1)
                        v.wait_ge(S("e_silu"), e * UNITS_E + (ge * UNITS_E + u + 1))
                        v.tensor_tensor(eact[:, u % 2, :], eact[:, u % 2, :], bank[:, u % 2, UNIT:2 * UNIT],
                                        ALU.mult).then_inc(S("e_act"), 1)
                        if u + 1 < UNITS_E:
                            part("b", u + 1)
                        if u >= 1:
                            act_low(u - 1)
                            part("d", u - 1)
                        if u == 2:
                            v.wait_ge(S("back_T"), e + (ge + 1))
                            pick_of(e + 1, lambda m: e * 3 + (3 * pe0 + 3 + m), e + (pe0 + 2))
                    act_low(UNITS_E - 1)
                    part("d", UNITS_E - 1)
                    v.tensor_copy(gcol[:, :], route[:, bass.ds(e, 1), :].rearrange("p a b -> p (a b)")
                                  ).then_inc(S("gcol_ready"), 1)
                    for h in range(2):
                        v.wait_ge(S("out_high"), e * 2 + (2 * ge + h + 1))
                        v.tensor_tensor(outL[:, h * 512:(h + 1) * 512], bank[:, 4 + h, :],
                                        outH[:, h * 512:(h + 1) * 512].bitcast(F32), ALU.subtract).then_inc(
                                            S("out_low"), 1)
                    v.wait_ge(S("gcol_ready"), e + (ge + 1))
                    for tt in range(TILES):
                        for h in range(2):
                            i = 2 * tt + h
                            ys = xhat[:, tt, h * 512:(h + 1) * 512]
                            v.wait_ge(S("scattered"), e * 4 + (4 * ge + i + 1))
                            v.scalar_tensor_tensor(ys, bank[:, 6 + h, :], gcol[:, 2 + tt:3 + tt], ys, ALU.mult,
                                                   ALU.add).then_inc(S("y_part"), 1)
                    v.wait_ge(S("y_part"), e * 4 + (4 * ge + 5))

            experts(N_DENSE, 0)
            most = v.value_load(flag[0:1, 0:1], min_val=0, max_val=TILES * P)
            with v.If(most > P):
                experts(N_DENSE + EXPERTS * PER_E, 1)
            for tt in range(TILES):
                st.do(v.tensor_tensor(xhat[:, tt, :], xhat[:, tt, :], gate[:, tt, :], ALU.mult), "y_gated")
                st.do(v.tensor_tensor(x[:, tt, :], x[:, tt, :], xhat[:, tt, :], ALU.add),
                      "y_ready" if tt == 1 else "y_gated")

        @block.tensor
        def _(pe):
            st = Steps(pe)

            def taken(n):
                pe.wait_ge(S("low_ready"), n + 1)

            def mm3(out, xh, xl, wh, wl, start, stop):
                pe.matmul(out, xh, wh, start=start, stop=False)
                pe.matmul(out, xh, wl, start=False, stop=False)
                return pe.matmul(out, xl, wh, start=False, stop=stop)

            ada_n, ada_outs = [0], [0]

            def ada(chunks):
                for l, c in chunks:
                    if ada_outs[0]:
                        pe.wait_ge(S("ada_out"), ada_outs[0])
                    for kh in range(2):
                        n = NUM[("ada", (l, c), kh)]
                        taken(n)
                        for k in range(KH):
                            for ring in (high, low):
                                w = w_slot(ring, n % SPLITS, (KH, 512))[:, k, :]
                                last = pe.matmul(bank[0:4, 6, :], cH[:, kh * KH + k, :], w,
                                                 start=kh == 0 and k == 0 and ring is high,
                                                 stop=kh == 1 and k == KH - 1 and ring is low)
                        last.then_inc(S("piece_used"), 1)
                    ada_n[0] += 1
                    pe.wait_ge(S("ada4_ready"), ada_n[0])
                    if c // 2 in (2, 5):
                        for tt in range(TILES):
                            last = pe.matmul(bank[:, 7 if tt == 0 else 6, :],
                                             const[0:4, C_SUMB + tt * P:C_SUMB + (tt + 1) * P], ada4[:, :],
                                             start=True, stop=True)
                    else:
                        for k in range(4):
                            last = pe.matmul(bank[:, 7, 2 * k:2 * k + 2], ada4[:, k * P:(k + 1) * P],
                                             const[0:4, C_SUM2:C_SUM2 + 2], start=True, stop=True)
                    st.mark(last, "ada_summed")
                    ada_outs[0] += 2 if c // 2 in (2, 5) else 1

            def transpose_x(i):
                pe.wait_ge(S("xhat_ready"), 2 * i + 2)
                for tt in range(TILES):
                    for k in range(KT):
                        last = pe.transpose(bank[:, 2 * tt + k // 4, (k % 4) * P:(k % 4 + 1) * P],
                                            xhat[:, tt, k * P:(k + 1) * P], ident)
                st.mark(last, "xhat_T")

            def linear(pieces, cw, out_bank):
                for kh, piece in enumerate(pieces):
                    n = NUM[piece]
                    taken(n)
                    for k in range(KH):
                        kk = kh * KH + k
                        for tt in range(TILES):
                            sl = slice(tt * P, (tt + 1) * P)
                            last = mm3(bank[:, out_bank(tt), 0:cw], hidH[:, kk, sl], hidL[:, kk, sl],
                                       w_slot(high, n % SPLITS, (KH, cw))[:, k, :],
                                       w_slot(low, n % SPLITS, (KH, cw))[:, k, :], kk == 0, kk == KT - 1)
                    last.then_inc(S("piece_used"), 1)
                return n

            pe.wait_ge(S("const_in"), 16)
            pe.wait_ge(S("rows_in"), 16 * 13)
            pe.transpose(bank[:, 7, 0:NROWS], prow[0:NROWS, 0, :], ident[0:NROWS, 0:NROWS])
            pe.transpose(bank[:, 6, 0:96], prow[0:96, 1, :], ident[0:96, 0:96])
            for half in range(2):
                last = pe.transpose(bank[:, 6, 96 + half * 124:96 + (half + 1) * 124], prow[0:124, 2 + half, :],
                                    ident[0:124, 0:124])
            st.mark(last, "rows_T")
            transpose_x(0)
            pe.wait_ge(S("c_low"), 1)
            pe.wait_ge(S("rows_out"), 3)
            ada(ADA_FIRST)
            pe.wait_ge(S("hid_ready"), 2)
            pe.wait_ge(S("hid_low"), 2)
            linear([("win", 0, 0), ("win", 0, 1)], Z0, lambda tt: tt)
            linear([("win", 2, 0), ("win", 2, 1)], SC, lambda tt: 2 + tt)
            pe.wait_ge(S("qlat_ready"), 2)
            for tt in range(TILES):
                for c in range(2):
                    pe.transpose(bank[:, 4, (2 * tt + c) * P:(2 * tt + c + 1) * P],
                                 z0[:, tt, c * P:(c + 1) * P], ident)
            pe.wait_ge(S("ckv_ready"), 2)
            for j in range(3):
                last = pe.transpose(bank[:, 5, j * P:(j + 1) * P], kv_lat[:, j, :], ident)
            st.mark(last, "lat_T")
            pe.wait_ge(S("lat_low"), 3)
            pe.wait_ge(S("gc_ready"), 2)
            n = NUM[("qb",)]
            taken(n)
            for tt in range(TILES):
                for hh in range(2):
                    for c in range(2):
                        cols = slice(hh * 4 * QK, (hh + 1) * 4 * QK)
                        sl = slice(tt * P, (tt + 1) * P)
                        last = mm3(bank[:, 2 * tt + hh, 0:4 * QK], upH[:, 0, c, sl], upL[:, 0, c, sl],
                                   w_slot(high, n % SPLITS, (2, HEADS * QK))[:, c, cols],
                                   w_slot(low, n % SPLITS, (2, HEADS * QK))[:, c, cols], c == 0, c == 1)
                if tt == 0:
                    st.mark(last, "q_product")
            last.then_inc(S("piece_used"), 1)
            n = NUM[("kvb",)]
            taken(n)
            ckvH = upH[:, 1, :, :].rearrange("p c n -> p (c n)")
            ckvL = upL[:, 1, :, :].rearrange("p c n -> p (c n)")

            def keys_values(j):
                b0 = (4, 0, 2)[j]
                if j:
                    pe.wait_ge(S("heads_in"), j)
                for hh in range(2):
                    last = mm3(bank[:, b0 + hh, :], ckvH[:, j * P:(j + 1) * P], ckvL[:, j * P:(j + 1) * P],
                               high[:, n % SPLITS, hh * 512:(hh + 1) * 512],
                               low[:, n % SPLITS, hh * 512:(hh + 1) * 512], True, True)
                if j < 2:
                    st.mark(last, "kv_product")
                else:
                    last.then_inc(S("piece_used"), 1)

            def heads_transposed(i):
                pe.wait_ge(S("heads_normed"), i + 1)
                if i:
                    pe.wait_ge(S("heads_out"), i)
                for h in range(HEADS):
                    last = pe.transpose(bank[0:QK, 6 + h // 4, (h % 4) * P:(h % 4 + 1) * P],
                                        heads_raw[:, i % 2, h, :], ident)
                st.mark(last, "heads_T")

            keys_values(0)
            heads_transposed(0)
            keys_values(1)
            keys_values(2)
            heads_transposed(1)
            pe.wait_ge(S("heads_in"), 3)
            pe.wait_ge(S("vals_ready"), 1)
            linear([("win", 3, 0), ("win", 3, 1)], SC, lambda tt: 4 + tt)
            heads_transposed(2)
            pe.wait_ge(S("heads_in"), 4)
            pe.wait_ge(S("vals_ready"), 2)
            linear([("win", 1, 0), ("win", 1, 1)], SC, lambda tt: tt)
            heads_transposed(3)
            heads_transposed(4)
            pe.wait_ge(S("v_ready"), 2)
            pe.wait_ge(S("gb_ready"), 2)
            pe.wait_ge(S("heads_in"), 5)
            pe.wait_ge(S("vals_ready"), 3)
            for w in range(2):
                for tt in range(TILES):
                    for c in range(SCC):
                        last = pe.transpose(bank[:, 2 * w + tt, c * P:(c + 1) * P],
                                            stage[:, w, tt, c * P:(c + 1) * P], ident)
            st.mark(last, "sc_T")
            pe.wait_ge(S("heads_out"), 5)
            pe.wait_ge(S("vT_ready"), 2)
            for h in range(HEADS):
                last = pe.matmul(bank[:, h // 4, (h % 4) * P:(h % 4 + 1) * P], qT[:, 0, h, :], kT[:, 0, h, :],
                                 start=True, stop=True)
            st.mark(last, "scores")
            pe.wait_ge(S("gbT_ready"), 2)
            for h in range(HEADS):
                for j, src in enumerate((2, 1)):
                    c0 = (h % 2) * 256 + j * P
                    last = pe.matmul(bank[:, 2 + h // 2, c0:c0 + P], qT[:, 1, h, :], kT[:, src, h, :],
                                     start=True, stop=True)
            st.mark(last, "scores")

            def prob_T(g):
                pe.wait_ge(S("prob_ready"), 1 if g < 2 else 2)
                if g >= 2:
                    pe.wait_ge(S("probT_ready"), g - 1)
                for m in range(4):
                    if g < 2:
                        src = prob_c[:, 4 * g + m, :]
                    else:
                        hh, j = divmod(4 * (g - 2) + m, 2)
                        src = prob_l[:, hh, j * P:(j + 1) * P]
                    last = pe.transpose(bank[:, g % 2, m * P:(m + 1) * P], src, ident)
                st.mark(last, "prob_T")

            def times_values(g):
                pe.wait_ge(S("probT_ready"), g + 1)
                for m in range(4):
                    if g < 2:
                        h, j, tt, kv = 4 * g + m, 0, 0, 0
                        start = stop = True
                    else:
                        h, j = divmod(4 * (g - 2) + m, 2)
                        tt, kv = 1, (2, 1)[j]
                        start, stop = j == 0, j == 1
                    p0 = (h % 2) * VH
                    last = pe.matmul(bank[p0:p0 + VH, 2 + tt, (h // 2) * P:(h // 2 + 1) * P],
                                     vals[:, kv, h, :], probT[:, g % 2, m, :], start=start, stop=stop)
                st.mark(last, "pv_group")

            pe.wait_ge(S("exp_c"), HEADS)
            prob_T(0)
            prob_T(1)
            pe.wait_ge(S("exp_l"), HEADS)
            times_values(0)
            prob_T(2)
            times_values(1)
            prob_T(3)
            times_values(2)
            prob_T(4)
            times_values(3)
            prob_T(5)
            times_values(4)
            times_values(5)
            ada(ADA_ATTN)
            ada(ADA_GATE[0])
            pe.wait_ge(S("hid_low"), 6)
            linear([("wo", 0, 0), ("wo", 0, 1)], 512, lambda tt: 2 + 2 * tt)
            linear([("wo", 1, 0), ("wo", 1, 1)], 512, lambda tt: 3 + 2 * tt)
            transpose_x(1)
            ada(ADA_GATE[1])
            pe.wait_ge(S("hid_low"), 8)

            def gate_up(u, kh, n, units_before):
                taken(n)
                for k in range(KH):
                    kk = kh * KH + k
                    for tt in range(TILES):
                        sl = slice(tt * P, (tt + 1) * P)
                        last = mm3(bank[:, tt, :], hidH[:, kk, sl], hidL[:, kk, sl],
                                   w_slot(high, n % SPLITS, (KH, 512))[:, k, :],
                                   w_slot(low, n % SPLITS, (KH, 512))[:, k, :], kk == 0, kk == KT - 1)
                last.then_inc(S("piece_used"), 1)

            n_units = D_FF // UNIT

            def ffn_T(u):
                pe.wait_ge(S("ffn_act"), TILES * (u + 1))
                if u:
                    pe.wait_ge(S("ffn_low"), UC * u)
                for tt in range(TILES):
                    for c in range(UC):
                        last = pe.transpose(bank[:, 6, (UC * tt + c) * P:(UC * tt + c + 1) * P],
                                            act[:, u % 2, tt, c * P:(c + 1) * P], ident)
                st.mark(last, "ffn_T")

            def ffn_down(u):
                n = NUM[("ffn", "d", u)]
                taken(n)
                pe.wait_ge(S("ffn_low"), UC * (u + 1))
                for c in range(UC):
                    for tt in range(TILES):
                        for h in range(2):
                            sl = slice(tt * P, (tt + 1) * P)
                            last = mm3(bank[:, 2 + 2 * tt + h, :], upH[:, u % 2, c, sl], upL[:, u % 2, c, sl],
                                       w_slot(high, n % SPLITS, (UC, D))[:, c, h * 512:(h + 1) * 512],
                                       w_slot(low, n % SPLITS, (UC, D))[:, c, h * 512:(h + 1) * 512],
                                       u == 0 and c == 0, u == n_units - 1 and c == UC - 1)
                last.then_inc(S("piece_used"), 1)
                return n

            for u in range(n_units):
                if u:
                    pe.wait_ge(S("ffn_act"), TILES * u)
                gate_up(u, 0, NUM[("ffn", "a", u)], 0)
                gate_up(u, 1, NUM[("ffn", "b", u)], 0)
                if u >= 1:
                    ffn_T(u - 1)
                if u >= 2:
                    ffn_down(u - 2)
            ffn_down(n_units - 2)
            ffn_T(n_units - 1)
            ffn_down(n_units - 1)
            transpose_x(2)
            ada(ADA_GATE[2])
            pe.wait_ge(S("hid_low"), 10)
            for u in range(4):
                if u >= 2:
                    pe.wait_ge(S("ag_ready"), TILES * (u - 1))
                for kh in range(2):
                    n = NUM[("pw1", "ab"[kh], u)]
                    taken(n)
                    for k in range(KH):
                        kk = kh * KH + k
                        for tt in range(TILES):
                            sl = slice(tt * P, (tt + 1) * P)
                            last = mm3(bank[:, 2 * (u % 2) + tt, :], hidH[:, kk, sl], hidL[:, kk, sl],
                                       w_slot(high, n % SPLITS, (KH, 512))[:, k, :],
                                       w_slot(low, n % SPLITS, (KH, 512))[:, k, :], kk == 0, kk == KT - 1)
                    last.then_inc(S("piece_used"), 1)
                pe.wait_ge(S("ag_ready"), TILES * (u + 1))
                if u:
                    pe.wait_ge(S("glu_ready"), UC * u)
                for tt in range(TILES):
                    for j in range(2 * UC):
                        last = pe.transpose(bank[:, 4 + tt, j * P:(j + 1) * P],
                                            ag[:, u % 2, tt, j * P:(j + 1) * P], ident)
                st.mark(last, "pw1_T")
            for k in range(KT):
                pe.wait_ge(S("conv_ready"), k + 1)
                last = pe.matmul(bank[:, 0, 0:TILES * P], const[:, C_ONES:C_ONES + P], hid[:, k, :],
                                 start=k == 0, stop=k == KT - 1)
            st.mark(last, "ln_sum")
            pe.wait_ge(S("sq_ready"), 1)
            for k in range(KT):
                last = pe.matmul(bank[:, 1, 0:TILES * P], const[:, C_ONES:C_ONES + P], sq[:, k, :],
                                 start=k == 0, stop=k == KT - 1)
            st.mark(last, "ln_sum")
            pe.wait_ge(S("glu_ready"), KT)
            pe.wait_ge(S("pw2_bias_in"), 16)
            for tt in range(TILES):
                for h in range(2):
                    pe.matmul(bank[:, 2 + 2 * tt + h, :], const[0:1, C_ONES:C_ONES + P],
                              pw2_b[0:1, h * 512:(h + 1) * 512], start=True, stop=False)
            pe.wait_ge(S("hid_low"), 12)
            for h in range(2):
                for kh in range(2):
                    n = NUM[("pw2", h, kh)]
                    taken(n)
                    for k in range(KH):
                        kk = kh * KH + k
                        for tt in range(TILES):
                            sl = slice(tt * P, (tt + 1) * P)
                            last = mm3(bank[:, 2 + 2 * tt + h, :], hidH[:, kk, sl], hidL[:, kk, sl],
                                       w_slot(high, n % SPLITS, (KH, 512))[:, k, :],
                                       w_slot(low, n % SPLITS, (KH, 512))[:, k, :], False, kk == KT - 1)
                    last.then_inc(S("piece_used"), 1)
            transpose_x(3)
            ada(ADA_GATE[3])
            pe.wait_ge(S("hid_ready"), 8)
            pe.wait_ge(S("router_in"), 16)
            for tt in range(TILES):
                for k in range(KT):
                    last = pe.matmul(bank[:, 4, tt * EXPERTS:(tt + 1) * EXPERTS], hid[:, k, tt * P:(tt + 1) * P],
                                     router_w[:, k, :], start=k == 0, stop=k == KT - 1)
            st.mark(last, "logits")
            for tt in range(TILES):
                for k in range(KT):
                    last = pe.transpose(bank[:, 2 * tt + k // 4, (k % 4) * P:(k % 4 + 1) * P],
                                        hid[:, k, tt * P:(tt + 1) * P], ident)
                st.mark(last, "tok_T")
            pe.wait_ge(S("chosen"), 1)
            M = 7
            before = const[:, C_BEFORE:C_BEFORE + P]
            ones = const[:, C_ONES:C_ONES + P]
            pe.matmul(bank[:, 5, 0:EXPERTS], before, rt[:, M, 0], start=True, stop=True)
            pe.matmul(bank[:, 5, EXPERTS:2 * EXPERTS], ones, rt[:, M, 0], start=True, stop=False)
            pe.matmul(bank[:, 5, EXPERTS:2 * EXPERTS], before, rt[:, M, 1], start=False, stop=True)
            pe.matmul(bank[:, 5, 2 * EXPERTS:3 * EXPERTS], ones, rt[:, M, 0], start=True, stop=False)
            st.mark(pe.matmul(bank[:, 5, 2 * EXPERTS:3 * EXPERTS], ones, rt[:, M, 1], start=False, stop=True),
                    "slots")
            pe.wait_ge(S("tok_low"), TILES)
            pe.wait_ge(S("flag_ready"), 1)

            def experts(first, passes):
                ge = passes * EXPERTS

                def gather(picked, slot_base, y_base):
                    pe.wait_ge(S("pickR_ready"), picked)
                    if y_base is not None:
                        pe.wait_ge(S("y_part"), y_base)
                    for part, src in enumerate((tokH, tokL)):
                        for kh in range(2):
                            if part:
                                pe.wait_ge(S("slot_ready"), slot_base + kh + 1)
                            for k in range(KH):
                                kk = kh * KH + k
                                for tt in range(TILES):
                                    last = pe.matmul(bank[:, 6 + kh, k * P:(k + 1) * P],
                                                     src[:, tt, kk * P:(kk + 1) * P], pickR[:, tt, :],
                                                     start=tt == 0, stop=tt == TILES - 1)
                            last.then_inc(S("gathered"), 1)

                g0 = passes * 4 * (EXPERTS + 1)
                gather(1 + passes * (EXPERTS + 1), g0, 4 * ge + 1)
                with pe.Fori(0, EXPERTS) as e:
                    def ready(n):
                        pe.wait_ge(S("low_ready"), e * PER_E + (n + 1))

                    def e_T(u):
                        pe.wait_ge(S("e_act"), e * UNITS_E + (ge * UNITS_E + u + 1))
                        if u >= 2:
                            pe.wait_ge(S("e_low"), e * UNITS_E + (ge * UNITS_E + u - 1))
                        for c in range(UC):
                            last = pe.transpose(bank[:, 2 + u % 2, c * P:(c + 1) * P],
                                                eact[:, u % 2, c * P:(c + 1) * P], ident)
                        last.then_inc(S("e_T"), 1)

                    def e_down(u):
                        n = first + NUM_E[("d", u)]
                        ready(n)
                        pe.wait_ge(S("e_low"), e * UNITS_E + (ge * UNITS_E + u + 1))
                        for c in range(UC):
                            for h in range(2):
                                last = mm3(bank[:, 4 + h, :], upH[:, u % 2, c, 0:P], upL[:, u % 2, c, 0:P],
                                           w_slot(high, n % SPLITS, (UC, D))[:, c, h * 512:(h + 1) * 512],
                                           w_slot(low, n % SPLITS, (UC, D))[:, c, h * 512:(h + 1) * 512],
                                           u == 0 and c == 0, u == UNITS_E - 1 and c == UC - 1)
                        last.then_inc(S("piece_used"), 1)

                    for u in range(UNITS_E):
                        if u == 0:
                            pe.wait_ge(S("slot_ready"), e * 4 + (g0 + 4))
                        for kh, kind in enumerate("ab"):
                            n = first + NUM_E[(kind, u)]
                            ready(n)
                            for k in range(KH):
                                kk = kh * KH + k
                                last = mm3(bank[:, u % 2, :], slotH[:, kk, :], slotL[:, kk, :],
                                           w_slot(high, n % SPLITS, (KH, 512))[:, k, :],
                                           w_slot(low, n % SPLITS, (KH, 512))[:, k, :], kk == 0, kk == KT - 1)
                            last.then_inc(S("piece_used"), 1)
                        if u == 0:
                            pe.wait_ge(S("y_part"), e * 4 + (4 * ge + 1))
                            for tt in range(TILES):
                                last = pe.transpose(bank[:, 6, tt * P:(tt + 1) * P], pick[:, tt, :], ident)
                            last.then_inc(S("back_T"), 1)
                        if u >= 1:
                            e_T(u - 1)
                        if u >= 2:
                            e_down(u - 2)
                    pe.wait_ge(S("back_ready"), e + (ge + 1))
                    gather(e + (2 + passes * (EXPERTS + 1)), e * 4 + (g0 + 4), None)
                    e_down(UNITS_E - 2)
                    e_T(UNITS_E - 1)
                    e_down(UNITS_E - 1)
                    pe.wait_ge(S("slot_ready"), e * 4 + (g0 + 8))
                    for tt in range(TILES):
                        for h in range(2):
                            if tt == 0:
                                pe.wait_ge(S("out_low"), e * 2 + (2 * ge + h + 1))
                            else:
                                pe.wait_ge(S("y_part"), e * 4 + (4 * ge + h + 2))
                            pe.matmul(bank[:, 6 + h, :], backR[:, tt, :], outH[:, h * 512:(h + 1) * 512],
                                      start=True, stop=False)
                            pe.matmul(bank[:, 6 + h, :], backR[:, tt, :], outL[:, h * 512:(h + 1) * 512],
                                      start=False, stop=True).then_inc(S("scattered"), 1)

            experts(N_DENSE, 0)
            most = pe.value_load(flag[0:1, 0:1], min_val=0, max_val=TILES * P)
            with pe.If(most > P):
                experts(N_DENSE + EXPERTS * PER_E, 1)


NAMES = ["x_prompt", "x_sample", "cache_ckv", "cache_kpe", "c", "c_ctx", "ada_w", "ada_b", "norm_mix", "norm_ffn",
         "w_in", "q_a_norm", "w_qb", "kv_a_norm", "w_kvb", "q_norm", "k_norm", "w_sc", "w_o", "ffn_gu", "ffn_down",
         "conv_pw1", "conv_pw1_b", "conv_dw", "conv_dw_b", "conv_ln_g", "conv_ln_b", "conv_pw2", "conv_pw2_b",
         "router", "moe_gu", "moe_down"]


def constants():
    import numpy as np
    c = np.zeros((P, C_END), np.float32)
    i = np.arange(P)
    c[:, C_ID:C_ID + P] = np.eye(P)
    c[:, C_BEFORE:C_BEFORE + P] = i[:, None] < i[None, :]
    c[:, C_ONES:C_ONES + P] = 1.0
    c[:, C_IOTA:C_IOTA + P] = i[None, :]
    grid_w = 64
    nf = ROPE // 4
    inv = (np.float32(10000.0) ** (-np.arange(nf, dtype=np.float32) / np.float32(nf))).astype(np.float32)
    for axis, pos in enumerate((i // grid_w, i % grid_w)):
        ang = pos[:, None].astype(np.float32) * inv[None, :]
        for s in range(2):
            d0 = (2 * axis + s) * nf
            for h in range(HEADS):
                c[:, C_COS + h * ROPE + d0:C_COS + h * ROPE + d0 + nf] = np.cos(ang)
                c[:, C_SIN + h * ROPE + d0:C_SIN + h * ROPE + d0 + nf] = np.sin(ang) * (-1.0 if s == 0 else 1.0)
    for row in range(4):
        c[row, C_SUM2 + row % 2] = 1.0
        c[row, C_SUMB + (row % 2) * P:C_SUMB + (row % 2 + 1) * P] = 1.0
    return c


def kernel(**inputs):
    import numpy as np
    import concourse.bacc as bacc
    from concourse.bass_utils import run_bass_kernel_spmd

    nc = bacc.Bacc("TRN2", target_bir_lowering=False, num_devices=1)
    arrays = {name: np.ascontiguousarray(inputs[name]) for name in NAMES}
    arrays["table"] = constants()
    t = {name: nc.dram_tensor(name, arr.shape, F32, kind="ExternalInput").ap() for name, arr in arrays.items()}
    shapes = [(1, P, D), (1, P, D), (1, 1, P, KV_LORA), (1, 1, P, ROPE)]
    outs = [nc.dram_tensor(f"out{i}", s, F32, kind="ExternalOutput").ap() for i, s in enumerate(shapes)]
    build(nc, t, outs)
    r = run_bass_kernel_spmd(nc, [arrays], core_ids=[0])
    return tuple(r.results[0][f"out{i}"] for i in range(4))
```

```python
import concourse.bass as bass
from concourse import mybir
from contextlib import ExitStack

F32 = mybir.dt.float32
F32R = mybir.dt.float32r
I32 = mybir.dt.int32
ALU = mybir.AluOpType
ACT = mybir.ActivationFunctionType
AX = mybir.AxisListType.X

P = 128
D = 1024
KT = D // P
KH = KT // 2
TILES = 2
HEADS, NOPE, ROPE, VH = 8, 64, 32, 64
QK = NOPE + ROPE
Q_LORA, KV_LORA = 256, 128
SC = 512
SCC = SC // P
TAPS = 31
PAD = TAPS // 2
D_FF, D_FFE, EXPERTS = 2816, 3584, 8
UNIT = 256
UC = UNIT // P
EPS = 1e-6
SCALE = float(QK) ** -0.5
Z0 = Q_LORA + KV_LORA + ROPE
RAWS = 6
SPLITS = 3
DIAGS = 6
PIECE = 2048

C_ID, C_BEFORE, C_ONES, C_IOTA = 0, P, 2 * P, 3 * P
C_COS = 4 * P
C_SIN = C_COS + HEADS * ROPE
C_SUM2 = C_SIN + HEADS * ROPE
C_SUMB = C_SUM2 + 2
C_END = C_SUMB + 2 * P

ROWS = {}
_r = 0
for _name, _n in (("c_ctx", 8), ("c", 8), ("norm_mix", 16), ("norm_ffn", 16), ("pw1_b", 16), ("dw_b", 8),
                  ("ln_g", 8), ("ln_b", 8), ("w_sc", 12), ("q_a", 2)):
    ROWS[_name] = _r
    _r += _n
NROWS = _r

ADA_FIRST = [(0, 2), (0, 3), (0, 0), (0, 1)]
ADA_ATTN = [(0, 8), (0, 9), (0, 6), (0, 7), (1, 2), (1, 3), (1, 0), (1, 1)]
ADA_CONV = [(1, 8), (1, 9), (1, 6), (1, 7)]
ADA_GATE = [[(0, 4), (0, 5)], [(0, 10), (0, 11)], [(1, 4), (1, 5)], [(1, 10), (1, 11)]]
DVE_TILES = 5


def ffn_stream(units):
    out = []
    for u in range(units):
        out += [("a", u), ("b", u)]
        if u >= 2:
            out.append(("d", u - 2))
    return out + [("d", units - 2), ("d", units - 1)]


def plan():
    order = []

    def ada(chunks):
        for c in chunks:
            order.extend([("ada", c, 0), ("ada", c, 1)])

    def win(c):
        order.extend([("win", c, 0), ("win", c, 1)])

    ada(ADA_FIRST)
    win(0)
    win(2)
    ada(ADA_ATTN[0:1])
    order.append(("qb",))
    ada(ADA_ATTN[1:2])
    order.append(("kvb",))
    ada(ADA_ATTN[2:3])
    win(3)
    ada(ADA_ATTN[3:4])
    win(1)
    ada(ADA_ATTN[4:])
    ada(ADA_GATE[0])
    order.extend([("wo", h, kh) for h in (0, 1) for kh in (0, 1)])
    ada(ADA_GATE[1])
    order.extend([("ffn", k, u) for k, u in ffn_stream(D_FF // UNIT)])
    order.extend([("pw1", k, u) for u in range(4) for k in "ab"])
    ada(ADA_CONV)
    ada(ADA_GATE[2])
    order.extend([("pw2", h, kh) for h in (0, 1) for kh in (0, 1)])
    ada(ADA_GATE[3])
    return order


ORDER = plan()
STREAM = {p: n for n, p in enumerate(ORDER)}
DIRECT = [p for p in ORDER if p[0] == "ada"]
SPLIT = [p for p in ORDER if p[0] != "ada"]
NUM = {p: n for n, p in enumerate(SPLIT)}
DNUM = {p: n for n, p in enumerate(DIRECT)}
N_DENSE = len(ORDER)
N_SPLIT = len(SPLIT)
UNITS_E = D_FFE // UNIT
STREAM_E = ffn_stream(UNITS_E)
NUM_E = {p: n for n, p in enumerate(STREAM_E)}
PER_E = len(STREAM_E)
assert PER_E % RAWS == 0 and PER_E % SPLITS == 0
W_CHUNK = {0: (0, Z0), 1: (Z0, SC), 2: (Z0 + SC, SC), 3: (Z0 + 2 * SC, SC)}


def build(nc, t, outs):
    ctx = ExitStack()
    with ctx:
        def sb(name, shape, dt=F32, where=None):
            return (where or ctx).enter_context(nc.sbuf_tensor(name, shape, dt))

        raw = sb("raw", [P, RAWS, PIECE])
        high = sb("high", [P, SPLITS, PIECE], F32R)
        low = sb("low", [P, SPLITS, PIECE], F32R)
        x = sb("x", [P, TILES, D])
        hid = sb("hid", [P, KT, TILES * P])
        hidH = sb("hidH", [P, KT, TILES * P], F32R)
        hidL = sb("hidL", [P, KT, TILES * P], F32R)
        gate = sb("gate", [P, TILES, D])
        upH = sb("upH", [P, 2, UC, TILES * P], F32R)
        upL = sb("upL", [P, 2, UC, TILES * P], F32R)
        const = sb("const", [P, C_END])
        par = sb("par", [P, NROWS])
        ada_bT = sb("ada_bT", [P, 2 * 48])
        taps = sb("taps", [P, TAPS * KT])
        cond = sb("cond", [P, KT, 32])
        mod = sb("mod", [P, 2, 4, KT, 2])
        aff = sb("aff", [P, KT, 2])
        ada4 = sb("ada4", [P, 512])
        small = sb("small", [P, 64])
        router_w = sb("router_w", [P, KT, EXPERTS])
        ph = ExitStack()
        z0 = sb("z0", [P, TILES, Z0], where=ph)
        kv_lat = sb("kv_lat", [P, 3, KV_LORA], where=ph)
        kpe_c = sb("kpe_c", [P, ROPE], where=ph)
        kv_gain = sb("kv_gain", [P, KV_LORA], where=ph)
        q_gain = sb("q_gain", [P, QK], where=ph)
        k_gain = sb("k_gain", [P, QK], where=ph)
        vals = sb("vals", [P, 3, HEADS, VH], where=ph)
        qT = sb("qT", [QK, TILES, HEADS, P], where=ph)
        kT = sb("kT", [QK, 3, HEADS, P], where=ph)
        work = sb("work", [P, 3 * HEADS * P], where=ph)
        probT = sb("probT", [P, 2, 4, P], where=ph)
        vTpad = sb("vTpad", [P, SCC, TILES, P + 2], where=ph)
        ph.close()
        ph = ExitStack()
        act = sb("act", [P, 2, TILES, UNIT], where=ph)
        ph.close()
        ph = ExitStack()
        ag = sb("ag", [P, 2, TILES, 512], where=ph)
        uT = sb("uT", [P, KT, TILES, P + 2 * PAD], where=ph)
        sg = sb("sg", [P, UC, TILES, P], where=ph)
        sq = sb("sq", [P, KT, TILES * P], where=ph)
        diag = sb("diag", [P, DIAGS, P], where=ph)
        stat = sb("stat", [P, 2, TILES * P], where=ph)
        pw2_b = sb("pw2_b", [1, D], where=ph)
        ph.close()
        ph = ExitStack()
        tokH = sb("tokH", [P, TILES, D], F32R, where=ph)
        tokL = sb("tokL", [P, TILES, D], F32R, where=ph)
        slotH = sb("slotH", [P, KT, P], F32R, where=ph)
        slotL = sb("slotL", [P, KT, P], F32R, where=ph)
        outH = sb("outH", [P, D], F32R, where=ph)
        outL = sb("outL", [P, D], F32R, where=ph)
        eact = sb("eact", [P, 2, UNIT], where=ph)
        pick = sb("pick", [P, TILES, P], where=ph)
        pickR = sb("pickR", [P, TILES, P], F32R, where=ph)
        backR = sb("backR", [P, TILES, P], F32R, where=ph)
        route = sb("route", [P, EXPERTS, 4], where=ph)
        rt = sb("rt", [P, 16, TILES, EXPERTS], where=ph)
        ecol = sb("ecol", [P, 4], where=ph)
        gcol = sb("gcol", [P, 4], where=ph)
        flag = sb("flag", [1, 1], I32, where=ph)
        ph.close()
        bank = ctx.enter_context(nc.psum_tensor("bank", [P, 8, 512], F32))

        ident = const[:, C_ID:C_ID + P]
        hid4 = hid[:, :, :].rearrange("p k (t n) -> p k t n", t=TILES)
        xhat = hid[:, :, :].rearrange("p k n -> p (k n)").rearrange("p (t d) -> p t d", t=TILES)
        stage = hid[:, :, :].rearrange("p k n -> p (k n)").rearrange("p (w t n) -> p w t n", w=2, t=TILES)
        gbT = gate[:, :, :].rearrange("p t d -> p (t d)")[:, 0:SCC * TILES * P].rearrange(
            "p (c t n) -> p c t n", c=SCC, t=TILES)
        heads_raw = work[:, 0:2 * HEADS * QK].rearrange("p (s h d) -> p s h d", s=2, h=HEADS)
        heads_sq = work[:, 2 * HEADS * QK:3 * HEADS * QK].rearrange("p (h d) -> p h d", h=HEADS)
        prow = work[:, 0:4 * P].rearrange("p (r n) -> p r n", r=4)
        prob_c = work[:, 0:HEADS * P].rearrange("p (h n) -> p h n", h=HEADS)
        prob_l = work[:, HEADS * P:].rearrange("p (h n) -> p h n", h=HEADS)
        rope_t = probT[:, 0, 0:2, :].rearrange("p a b -> p (a b)").rearrange("p (h d) -> p h d", h=HEADS)

        sems = {}

        def S(name):
            if name not in sems:
                sems[name] = ctx.enter_context(nc.semaphore(name))
            return sems[name]

        class Steps:

            def __init__(self, eng):
                self.eng, self.n = eng, {}

            def mark(self, ins, name):
                ins.then_inc(S(name), 1)
                self.n[name] = self.n.get(name, 0) + 1
                return self.n[name]

            def do(self, ins, name):
                self.eng.wait_ge(S(name), self.mark(ins, name))

        def cat(ap):
            return ap.rearrange("p a b -> p (a b)")

        def w_slot(ring, n, shape):
            size = 1
            for s in shape:
                size *= s
            v = ring[:, n, 0:size]
            if len(shape) == 2:
                return v.rearrange("p (a b) -> p a b", a=shape[0])
            if len(shape) == 3:
                return v.rearrange("p (a b c) -> p a b c", a=shape[0], b=shape[1])
            return v

        def width(piece):
            if piece[0] == "qb":
                return 2 * HEADS * QK
            if piece[0] == "kvb":
                return HEADS * (NOPE + VH)
            if piece[0] == "win" and piece[1] == 0:
                return KH * Z0
            return PIECE

        def gu_parts(w_gu, ff, u, kh):
            v = w_gu.rearrange("(h k p) n -> h p k n", p=P, k=KH)[kh]
            return v[:, :, u * UNIT:(u + 1) * UNIT], v[:, :, ff + u * UNIT:ff + (u + 1) * UNIT]

        def col_part(w, kh, c0, cw):
            return w.rearrange("(h k p) n -> h p k n", p=P, k=KH)[kh][:, :, c0:c0 + cw]

        def product(eng, *piece):
            eng.wait_ge(S("piece_used"), NUM[piece] + 1)

        block = ctx.enter_context(nc.Block())

        @block.sync
        def _(sp):
            def load(n, piece):
                slot, use = n % RAWS, n // RAWS
                arrived = S(f"raw_in{slot}")
                if n >= RAWS:
                    last = ORDER[n - RAWS]
                    if last in DNUM:
                        sp.wait_ge(S("direct_used"), DNUM[last] + 1)
                    else:
                        sp.wait_ge(S("low_ready"), NUM[last] + 1)
                kind = piece[0]
                if kind in ("ffn", "pw1") and piece[1] != "d":
                    w, ff = (t["ffn_gu"][0], D_FF) if kind == "ffn" else (t["conv_pw1"][0], D)
                    dst = w_slot(raw, slot, (KH, 2, UNIT))
                    g, u = gu_parts(w, ff, piece[2], "ab".index(piece[1]))
                    sp.dma_start(dst[:, :, 0, :], g).then_inc(arrived, 16)
                    sp.dma_start(dst[:, :, 1, :], u).then_inc(arrived, 16)
                    return 32
                if kind == "ffn":
                    dst = w_slot(raw, slot, (UC, D))
                    src = t["ffn_down"][0].rearrange("(u c p) n -> u p c n", p=P, c=UC)[piece[2]]
                elif kind == "ada":
                    (l, c), kh = piece[1], piece[2]
                    dst = w_slot(raw, slot, (KH, 512))
                    src = col_part(t["ada_w"][l], kh, c * 512, 512)
                elif kind == "win":
                    c0, cw = W_CHUNK[piece[1]]
                    dst = w_slot(raw, slot, (KH, cw))
                    src = col_part(t["w_in"][0], piece[2], c0, cw)
                elif kind == "qb":
                    dst = w_slot(raw, slot, (2, HEADS * QK))
                    src = t["w_qb"][0].rearrange("(k p) n -> p k n", p=P)
                elif kind == "kvb":
                    dst = w_slot(raw, slot, (1, D))
                    src = t["w_kvb"][0].rearrange("(k p) n -> p k n", p=P)
                else:
                    w = t["w_o"][0] if kind == "wo" else t["conv_pw2"][0]
                    dst = w_slot(raw, slot, (KH, 512))
                    src = col_part(w, piece[2], piece[1] * 512, 512)
                sp.dma_start(dst, src).then_inc(arrived, 16)
                return 16

            for n, piece in enumerate(ORDER):
                load(n, piece)

            def expert_load(e, first, i, free):
                kind, u = STREAM_E[i]
                slot = (first + i) % RAWS
                arrived = S(f"raw_in{slot}")
                free()
                if kind == "d":
                    src = t["moe_down"][0].rearrange("e (u c p) n -> e u p c n", p=P, c=UC)
                    sp.dma_start(w_slot(raw, slot, (UC, D)), src[bass.ds(e, 1), u]).then_inc(arrived, 16)
                else:
                    kh = "ab".index(kind)
                    v = t["moe_gu"][0].rearrange("e (h k p) n -> e h p k n", p=P, k=KH)[bass.ds(e, 1), kh]
                    dst = w_slot(raw, slot, (KH, 2, UNIT))
                    c0 = u * UNIT
                    sp.dma_start(dst[:, :, 0, :], v[:, :, :, c0:c0 + UNIT]).then_inc(arrived, 16)
                    sp.dma_start(dst[:, :, 1, :], v[:, :, :, D_FFE + c0:D_FFE + c0 + UNIT]).then_inc(arrived, 16)

            def experts(passes):
                first, split = N_DENSE + passes * EXPERTS * PER_E, N_SPLIT + passes * EXPERTS * PER_E

                def dense_free(i):
                    last = ORDER[first + i - RAWS]
                    if last in DNUM:
                        sp.wait_ge(S("direct_used"), DNUM[last] + 1)
                    else:
                        sp.wait_ge(S("low_ready"), NUM[last] + 1)

                lead = RAWS if passes == 0 else 0
                for i in range(lead):
                    expert_load(0, first, i, lambda: dense_free(i))
                for i in range(lead, PER_E if lead else 0):
                    expert_load(0, first, i, lambda: sp.wait_ge(S("low_ready"), split + i - RAWS + 1))
                with sp.Fori(1 if lead else 0, EXPERTS) as e:
                    for i in range(PER_E):
                        expert_load(e, first, i,
                                    lambda: sp.wait_ge(S("low_ready"), e * PER_E + (split + i - RAWS + 1)))

            experts(0)
            sp.wait_ge(S("flag_ready"), 1)
            most = sp.value_load(flag[0:1, 0:1], min_val=0, max_val=TILES * P)
            with sp.If(most > P):
                experts(1)
            sp.wait_ge(S("y_ready"), 1)
            sp.dma_start(outs[0][0], x[:, 0, :]).then_inc(S("y_out"), 16)
            sp.dma_start(outs[1][0], x[:, 1, :]).then_inc(S("y_out"), 16)
            sp.wait_ge(S("y_out"), 32)

        def loads_of(piece):
            return 2 if piece[0] in ("ffn", "pw1") and piece[1] != "d" else 1

        def arrived_value(n):
            return 16 * sum(loads_of(ORDER[m]) for m in range(n % RAWS, n + 1, RAWS))

        def slot_total(slot):
            return 16 * sum(loads_of(ORDER[m]) for m in range(slot, N_DENSE, RAWS))

        def expert_value(first, i):
            slot = (first + i) % RAWS
            within = sum(16 if STREAM_E[m][0] == "d" else 32 for m in range(i + 1) if (first + m) % RAWS == slot)
            per = sum(16 if STREAM_E[m][0] == "d" else 32 for m in range(PER_E) if (first + m) % RAWS == slot)
            passes = (first - N_DENSE) // (EXPERTS * PER_E)
            return slot_total(slot) + passes * EXPERTS * per + within, per

        @block.gpsimd
        def _(pool):
            st = Steps(pool)
            st.do(pool.memset(small[:, 48:64], -0.5), "exponent")

            def inverse_root(c0, cw, need):
                pool.wait_ge(S("ms_ready"), need)
                st.mark(pool.tensor_tensor(small[:, c0:c0 + cw], small[:, c0:c0 + cw], small[:, 48:48 + cw],
                                           ALU.pow), "rstd_ready")

            def gate_bias(i):
                l, c0 = i // 2, (2 if i % 2 == 0 else 5) * D
                src = t["ada_b"][l:l + 1, c0:c0 + D].partition_broadcast(P)
                if i == 0:
                    pool.wait_ge(S("sc_gated"), 1)
                else:
                    pool.wait_ge(S("residual"), 2 * i)
                for tt in range(TILES):
                    pool.dma_start(gate[:, tt, :], src).then_inc(S("gate_bias"), 16)

            inverse_root(0, 2, 1)
            inverse_root(0, 4, 2)
            pool.wait_ge(S("ckv_ready"), 2)
            pool.dma_start(outs[2][0, 0], kv_lat[:, 0, :]).then_inc(S("state_out"), 16)
            pool.dma_start(outs[3][0, 0], z0[:, 0, Q_LORA + KV_LORA:Z0]).then_inc(S("state_out"), 16)
            for i in range(5):
                inverse_root(0, HEADS, 3 + i)
            gate_bias(0)
            inverse_root(0, 2, 8)
            gate_bias(1)
            inverse_root(0, 2, 9)
            gate_bias(2)
            inverse_root(0, 2, 10)
            gate_bias(3)
            pool.wait_ge(S("state_out"), 32)

        @block.scalar
        def _(a):
            st = Steps(a)
            a.dma_start(const[:, :], t["table"]).then_inc(S("const_in"), 16)
            rows = {"c_ctx": t["c_ctx"].rearrange("(r f) -> r f", f=P),
                    "c": t["c"].rearrange("b (r f) -> (b r) f", f=P),
                    "norm_mix": t["norm_mix"].rearrange("l (r f) -> (l r) f", f=P),
                    "norm_ffn": t["norm_ffn"].rearrange("l (r f) -> (l r) f", f=P),
                    "pw1_b": t["conv_pw1_b"].rearrange("l (r f) -> (l r) f", f=P),
                    "dw_b": t["conv_dw_b"].rearrange("l (r f) -> (l r) f", f=P),
                    "ln_g": t["conv_ln_g"].rearrange("l (r f) -> (l r) f", f=P),
                    "ln_b": t["conv_ln_b"].rearrange("l (r f) -> (l r) f", f=P),
                    "w_sc": t["w_sc"][0].rearrange("j (r f) -> (j r) f", f=P),
                    "q_a": t["q_a_norm"].rearrange("l (r f) -> (l r) f", f=P)}
            for name, src in rows.items():
                a.dma_start(prow[ROWS[name]:ROWS[name] + src.shape[0], 0, :], src).then_inc(S("rows_in"), 16)
            a.dma_start(prow[0:96, 1, :], t["ada_b"].rearrange("l (r f) -> (l r) f", f=P)).then_inc(S("rows_in"), 16)
            for half in range(2):
                src = t["conv_dw"][0].rearrange("j (r f) -> (j r) f", f=P)[half * 124:(half + 1) * 124, :]
                a.dma_start(prow[0:124, 2 + half, :], src).then_inc(S("rows_in"), 16)
            a.dma_start(x[:, 0, :], t["x_prompt"][0]).then_inc(S("x_in"), 16)
            a.dma_start(x[:, 1, :], t["x_sample"][0]).then_inc(S("x_in"), 16)
            a.dma_start(kv_gain[:, :], t["kv_a_norm"].partition_broadcast(P)).then_inc(S("attn_in"), 16)
            a.dma_start(q_gain[:, :], t["q_norm"].partition_broadcast(P)).then_inc(S("attn_in"), 16)
            a.dma_start(k_gain[:, :], t["k_norm"].partition_broadcast(P)).then_inc(S("attn_in"), 16)
            a.dma_start(kv_lat[:, 2, :], t["cache_ckv"][0, 0]).then_inc(S("attn_in"), 16)
            a.dma_start(kpe_c[:, :], t["cache_kpe"][0, 0]).then_inc(S("attn_in"), 16)
            a.dma_start(router_w[:, :, :], t["router"][0].rearrange("(k p) n -> p k n", p=P)).then_inc(
                S("router_in"), 16)

            def high_part(n, w=PIECE):
                m = STREAM[SPLIT[n]]
                a.wait_ge(S(f"raw_in{m % RAWS}"), arrived_value(m))
                if n >= SPLITS:
                    a.wait_ge(S("piece_used"), n - SPLITS + 1)
                a.activation(high[:, n % SPLITS, 0:w], raw[:, m % RAWS, 0:w], ACT.Copy).then_inc(S("high_ready"), 1)

            def named(*piece):
                high_part(NUM[piece], width(piece))

            def squares(i):
                for tt in range(TILES):
                    if i:
                        a.wait_ge(S("residual"), 2 * i - 1 + tt)
                    elif tt == 0:
                        a.wait_ge(S("x_in"), 32)
                    st.mark(a.activation(xhat[:, tt, :], x[:, tt, :], ACT.Square,
                                         accum_out=small[:, 16 + tt:17 + tt]), "sum_sq")

            def modulate_latents(i):
                l, w = i // 2, i % 2
                a.wait_ge(S("xhat_T"), i + 1)
                a.wait_ge(S("aff_ready"), i + 1)
                for k in range(KT):
                    st.mark(a.activation(hid4[:, k, 1, :], bank[:, 2 + k // 4, (k % 4) * P:(k % 4 + 1) * P],
                                         ACT.Identity, bias=mod[:, l, 2 * w, k, 1:2], scale=aff[:, k, 1:2]),
                            "hid_lat")

            def hidden_high(i):
                for tt in range(TILES):
                    if tt == 0:
                        a.wait_ge(S("hid_ctx"), i + 1)
                    else:
                        a.wait_ge(S("hid_lat"), KT * (i + 1))
                    st.mark(a.activation(hidH[:, :, tt * P:(tt + 1) * P], hid4[:, :, tt, :], ACT.Copy),
                            "hid_high")

            squares(0)
            a.wait_ge(S("rows_T"), 1)
            a.wait_ge(S("cleared"), 1)
            st.mark(a.activation(cond[:, :, 0:2].rearrange("p k c -> p c k"),
                                 bank[:, 7, 0:16].rearrange("p (c k) -> p c k", c=2), ACT.Silu), "silu_c")
            named("win", 0, 0)
            modulate_latents(0)
            hidden_high(0)
            named("win", 0, 1)
            named("win", 2, 0)
            product(a, "win", 0, 1)
            for tt in range(TILES):
                st.mark(a.activation(z0[:, tt, :], bank[:, tt, 0:Z0], ACT.Copy), "z0_ready")
            named("win", 2, 1)
            product(a, "win", 2, 1)
            a.wait_ge(S("hid_low"), 2)
            for tt in range(TILES):
                st.mark(a.activation(stage[:, 0, tt, :], bank[:, 2 + tt, :], ACT.Copy), "gc_ready")
            named("qb")
            a.wait_ge(S("lat_T"), 1)
            for c in range(2):
                st.mark(a.activation(upH[:, 0, c, :].rearrange("p (t n) -> p t n", t=TILES),
                                     bank[:, 4, :].rearrange("p (t c n) -> p t c n", t=TILES, c=2)[:, :, c, :],
                                     ACT.Copy, scale=par[:, ROWS["q_a"] + c:ROWS["q_a"] + c + 1]), "lat_high")
            st.mark(a.activation(upH[:, 1, :, :].rearrange("p c n -> p (c n)")[:, 0:3 * P], bank[:, 5, 0:3 * P],
                                 ACT.Copy), "lat_high")
            named("kvb")
            named("win", 3, 0)

            def square_heads(i):
                a.wait_ge(S("heads_in"), i + 1)
                st.mark(a.activation(heads_sq, heads_raw[:, i % 2], ACT.Square), "heads_sq")

            def head_transposes_out(i):
                dst = qT[:, i] if i < 2 else kT[:, i - 2]
                for half in range(2):
                    a.wait_ge(S("heads_T"), 2 * i + half + 1)
                    st.mark(a.activation(cat(dst[:, half * 4:half * 4 + 4, :]), bank[0:QK, 7, :], ACT.Copy),
                            "heads_out")

            def values_out(i):
                b0 = (4, 0, 2)[i]
                a.wait_ge(S("heads_in"), 3 + i)
                src = cat(bank[:, b0:b0 + 2, :]).rearrange("p (h d) -> p h d", h=HEADS)[:, :, NOPE:]
                st.mark(a.activation(vals[:, i], src, ACT.Copy), "vals_ready")

            square_heads(0)
            square_heads(1)
            named("win", 3, 1)
            head_transposes_out(0)
            square_heads(2)
            values_out(0)
            named("win", 1, 0)
            head_transposes_out(1)
            square_heads(3)
            values_out(1)
            named("win", 1, 1)
            head_transposes_out(2)
            square_heads(4)
            values_out(2)
            product(a, "win", 1, 1)
            for tt in range(TILES):
                st.mark(a.activation(stage[:, 1, tt, :], bank[:, tt, :], ACT.Copy), "gb_ready")
            head_transposes_out(3)
            head_transposes_out(4)
            a.wait_ge(S("sc_T"), 1)
            for tt in range(TILES):
                st.mark(a.activation(gbT[:, :, tt, :], bank[:, 2 + tt, :].rearrange("p (c n) -> p c n", c=SCC),
                                     ACT.Copy), "gbT_ready")
            a.wait_ge(S("max_ready"), 1)
            for h in range(HEADS):
                st.mark(a.activation(prob_c[:, h, :], bank[:, h // 4, (h % 4) * P:(h % 4 + 1) * P], ACT.Exp,
                                     bias=small[:, 24 + h:25 + h], scale=SCALE,
                                     accum_out=small[:, 8 + h:9 + h]), "exp_c")
            a.wait_ge(S("max_ready"), 2)
            for h in range(HEADS):
                st.mark(a.activation(prob_l[:, h, :], bank[:, 2 + h // 2, (h % 2) * 256:(h % 2 + 1) * 256], ACT.Exp,
                                     bias=small[:, 32 + h:33 + h],
                                     scale=SCALE, accum_out=small[:, 16 + h:17 + h]), "exp_l")
            for g in range(6):
                a.wait_ge(S("prob_T"), g + 1)
                if g >= 2:
                    a.wait_ge(S("pv_group"), g - 1)
                st.mark(a.activation(cat(probT[:, g % 2]), bank[:, g % 2, :], ACT.Copy), "probT_ready")
            for tt in range(TILES):
                a.wait_ge(S("pv_group"), 2 if tt == 0 else 6)
                st.mark(a.activation(hidH[:, 0:4, tt * P:(tt + 1) * P],
                                     bank[:, 2 + tt, :].rearrange("p (c n) -> p c n", c=4), ACT.Copy), "hid_high")
            a.wait_ge(S("sc_gated"), 1)
            for tt in range(TILES):
                st.mark(a.activation(hidH[:, 4:8, tt * P:(tt + 1) * P], hid4[:, 4:8, tt, :], ACT.Copy), "hid_high")
            for h in (0, 1):
                named("wo", h, 0)
                named("wo", h, 1)
            squares(1)

            def unit_high(kind, u):
                named("ffn", kind, u)

            n_units = D_FF // UNIT
            unit_high("a", 0)
            unit_high("b", 0)
            modulate_latents(1)
            hidden_high(1)
            for u in range(n_units):
                if u + 1 < n_units:
                    unit_high("a", u + 1)
                product(a, "ffn", "b", u)
                if u >= 2:
                    a.wait_ge(S("ffn_T"), u - 1)
                for tt in range(TILES):
                    st.mark(a.activation(act[:, u % 2, tt, :], bank[:, tt, 0:UNIT], ACT.Silu), "ffn_silu")
                if u + 1 < n_units:
                    unit_high("b", u + 1)
                for v in ([u - 1] if u >= 1 else []) + ([u] if u + 1 == n_units else []):
                    a.wait_ge(S("ffn_T"), v + 1)
                    if v >= 2:
                        a.wait_ge(S("piece_used"), NUM[("ffn", "d", v - 2)] + 1)
                    src = bank[:, 6, :].rearrange("p (t c n) -> p c t n", t=TILES, c=UC)
                    st.mark(a.activation(upH[:, v % 2].rearrange("p c (t n) -> p c t n", t=TILES), src, ACT.Copy),
                            "ffn_high")
                    unit_high("d", v)
            squares(2)
            a.dma_start(pw2_b[:, :], t["conv_pw2_b"]).then_inc(S("pw2_bias_in"), 16)
            def glu_gate(u):
                a.wait_ge(S("pw1_T"), u + 1)
                if u:
                    a.wait_ge(S("glu_ready"), UC * u)
                for c in range(UC):
                    k = u * UC + c
                    src = bank[:, 4:6, (UC + c) * P:(UC + c + 1) * P]
                    st.mark(a.activation(sg[:, c], src, ACT.Sigmoid,
                                         bias=par[:, ROWS["pw1_b"] + KT + k:ROWS["pw1_b"] + KT + k + 1]),
                            "sg_ready")

            def conv_out(k):
                a.wait_ge(S("tap_used"), (k - DVE_TILES + 1) * TAPS)
                st.mark(a.activation(hid[:, k, :], bank[:, k % 2, 0:TILES * P], ACT.Identity,
                                     bias=par[:, ROWS["dw_b"] + k:ROWS["dw_b"] + k + 1]), "conv_pe_ready")

            named("pw1", "a", 0)
            named("pw1", "b", 0)
            modulate_latents(2)
            hidden_high(2)
            for u in range(4):
                if u < 3:
                    named("pw1", "a", u + 1)
                product(a, "pw1", "b", u)
                if u >= 2:
                    a.wait_ge(S("pw1_T"), u - 1)
                for tt in range(TILES):
                    st.mark(a.activation(ag[:, u % 2, tt, :], bank[:, 2 * (u % 2) + tt, :], ACT.Copy), "ag_ready")
                if u < 3:
                    named("pw1", "b", u + 1)
                if u >= 1:
                    glu_gate(u - 1)
            glu_gate(3)
            for k in range(DVE_TILES, KT):
                for j in range(TAPS):
                    i = (k - DVE_TILES) * TAPS + j
                    if i >= DIAGS:
                        a.wait_ge(S("tap_used"), i - DIAGS + 1)
                    st.mark(a.activation(diag[:, i % DIAGS, :], ident, ACT.Copy,
                                         scale=taps[:, j * KT + k:j * KT + k + 1]), "diag_ready")
                if k > DVE_TILES:
                    conv_out(k - 1)
            conv_out(KT - 1)
            named("pw2", 0, 0)
            named("pw2", 0, 1)
            named("pw2", 1, 0)
            a.wait_ge(S("centred"), 1)
            st.mark(a.activation(sq[:, :, :], hid[:, :, :], ACT.Square), "sq_ready")
            a.wait_ge(S("inv_var"), 1)
            st.mark(a.activation(stat[:, 1, :], stat[:, 0, :], ACT.Sqrt), "ln_rstd")
            a.wait_ge(S("ln_scaled"), 1)
            for k in range(KT):
                st.mark(a.activation(hid[:, k, :], hid[:, k, :], ACT.Silu,
                                   bias=par[:, ROWS["ln_b"] + k:ROWS["ln_b"] + k + 1],
                                   scale=par[:, ROWS["ln_g"] + k:ROWS["ln_g"] + k + 1]), "ln_silu")
            a.wait_ge(S("ln_silu"), KT)
            for tt in range(TILES):
                st.mark(a.activation(hidH[:, :, tt * P:(tt + 1) * P], hid4[:, :, tt, :], ACT.Copy), "hid_high")
            named("pw2", 1, 1)

            def first_expert(kind, u):
                i = NUM_E[(kind, u)]
                n, m = N_DENSE + i, N_SPLIT + i
                a.wait_ge(S(f"raw_in{n % RAWS}"), expert_value(N_DENSE, i)[0])
                a.wait_ge(S("piece_used"), m - SPLITS + 1)
                a.activation(high[:, m % SPLITS, :], raw[:, n % RAWS, :], ACT.Copy).then_inc(S("high_ready"), 1)

            first_expert("a", 0)
            squares(3)
            first_expert("b", 0)
            modulate_latents(3)
            first_expert("a", 1)
            for tt in range(TILES):
                a.wait_ge(S("tok_T"), tt + 1)
                st.mark(a.activation(tokH[:, tt, :], cat(bank[:, 2 * tt:2 * tt + 2, :]), ACT.Copy), "tok_high")
            a.wait_ge(S("top2_diff"), 1)
            st.mark(a.activation(small[:, 2:4], small[:, 0:2], ACT.Exp), "top2_exp")

            def experts(first, split, passes):
                ge = passes * EXPERTS

                def picked(e):
                    a.wait_ge(S("pick_ready"), e + (ge + 1))
                    a.activation(pickR[:, :, :], pick[:, :, :], ACT.Copy).then_inc(S("pickR_ready"), 1)

                def gather_out(e):
                    for part, dst in enumerate((slotH, slotL)):
                        for kh in range(2):
                            i = 2 * part + kh
                            a.wait_ge(S("gathered"), e * 4 + (4 * ge + i + 1))
                            a.activation(cat(dst[:, kh * KH:(kh + 1) * KH, :]), bank[:, (6, 0)[part] + kh, :],
                                         ACT.Copy).then_inc(S("slot_ready"), 1)

                def part(e, kind, u):
                    i = NUM_E[(kind, u)]
                    n, m = first + i, split + i
                    value, per = expert_value(first, i)
                    a.wait_ge(S(f"raw_in{n % RAWS}"), e * per + value)
                    a.wait_ge(S("piece_used"), e * PER_E + (m - SPLITS + 1))
                    a.activation(high[:, m % SPLITS, :], raw[:, n % RAWS, :], ACT.Copy).then_inc(S("high_ready"), 1)

                def silu(e, u):
                    a.wait_ge(S("piece_used"), e * PER_E + (split + NUM_E[("b", u)] + 1))
                    a.activation(eact[:, u % 2, :], bank[:, u % 2, 0:UNIT], ACT.Silu).then_inc(S("e_silu"), 1)

                def act_high(e, w):
                    a.wait_ge(S("e_T"), e * UNITS_E + (ge * UNITS_E + w + 1))
                    if w >= 2:
                        a.wait_ge(S("piece_used"), e * PER_E + (split + NUM_E[("d", w - 2)] + 1))
                    a.activation(upH[:, w % 2, :, 0:P], bank[:, 2 + w % 2, 0:UNIT].rearrange(
                        "p (c n) -> p c n", c=UC), ACT.Copy).then_inc(S("e_high"), 1)

                def start(e):
                    part(e, "b", 1)
                    silu(e, 0)

                def body(e, last):
                    for u in range(1, UNITS_E):
                        if u + 1 < UNITS_E:
                            part(e, "a", u + 1)
                        silu(e, u)
                        if u == 3:
                            a.wait_ge(S("back_T"), e + (ge + 1))
                            a.activation(cat(backR[:, :, :]), bank[:, 6, 0:TILES * P], ACT.Copy).then_inc(
                                S("back_ready"), 1)
                        if u + 1 < UNITS_E:
                            part(e, "b", u + 1)
                        act_high(e, u - 1)
                        part(e, "d", u - 1)
                        if u == 6 and not last:
                            picked(e + 1)
                    part(e, "d", UNITS_E - 1)
                    act_high(e, UNITS_E - 1)
                    if not last:
                        gather_out(e + 1)
                        part(e + 1, "a", 0)
                        part(e + 1, "b", 0)
                    for h in range(2):
                        a.wait_ge(S("piece_used"), e * PER_E + (split + PER_E))
                        a.activation(outH[:, h * 512:(h + 1) * 512], bank[:, 4 + h, :], ACT.Copy).then_inc(
                            S("out_high"), 1)
                    if not last:
                        part(e + 1, "a", 1)
                        start(e + 1)

                if passes:
                    part(0, "a", 0)
                    part(0, "b", 0)
                picked(0)
                gather_out(0)
                if passes:
                    part(0, "a", 1)
                start(0)
                with a.Fori(0, EXPERTS - 1) as e:
                    body(e, False)
                body(EXPERTS - 1, True)

            experts(N_DENSE, N_SPLIT, 0)
            a.wait_ge(S("flag_ready"), 1)
            most = a.value_load(flag[0:1, 0:1], min_val=0, max_val=TILES * P)
            with a.If(most > P):
                experts(N_DENSE + EXPERTS * PER_E, N_SPLIT + EXPERTS * PER_E, 1)

        @block.vector
        def _(v):
            st = Steps(v)

            def low_part(n, w=PIECE):
                v.wait_ge(S("high_ready"), n + 1)
                v.tensor_tensor(low[:, n % SPLITS, 0:w], raw[:, STREAM[SPLIT[n]] % RAWS, 0:w],
                                high[:, n % SPLITS, 0:w].bitcast(F32), ALU.subtract).then_inc(S("low_ready"), 1)

            def named(*piece):
                low_part(NUM[piece], width(piece))

            def mean_square(i):
                v.wait_ge(S("sum_sq"), 2 * i + 2)
                st.do(v.tensor_scalar(small[:, 0:2], small[:, 16:18], 1.0 / D, EPS, ALU.mult, ALU.add), "ms_ready")

            def rms_scale(ms_count):
                v.wait_ge(S("rstd_ready"), ms_count)
                for tt in range(TILES):
                    st.mark(v.tensor_scalar(xhat[:, tt, :], x[:, tt, :], small[:, tt:tt + 1], None, ALU.mult),
                            "xhat_ready")

            def gain_scale(i):
                l, w = i // 2, i % 2
                g0 = ROWS["norm_ffn" if w else "norm_mix"] + l * KT
                g = par[:, g0:g0 + KT].unsqueeze(2).to_broadcast([P, KT, 2])
                st.do(v.scalar_tensor_tensor(aff[:, :, :], mod[:, l, 2 * w + 1], 1.0, g, ALU.add, ALU.mult),
                      "aff_ready")

            def modulate_context(i):
                l, w = i // 2, i % 2
                v.wait_ge(S("xhat_T"), i + 1)
                for k in range(KT):
                    st.mark(v.tensor_scalar(hid4[:, k, 0, :], bank[:, k // 4, (k % 4) * P:(k % 4 + 1) * P],
                                            aff[:, k, 0:1], mod[:, l, 2 * w, k, 0:1], ALU.mult, ALU.add),
                            "hid_ctx" if k == KT - 1 else "hid_parts")

            def hidden_low(high_count):
                for tt in range(TILES):
                    v.wait_ge(S("hid_high"), high_count + tt + 1)
                    st.mark(v.tensor_tensor(hidL[:, :, tt * P:(tt + 1) * P], hid4[:, :, tt, :],
                                            hidH[:, :, tt * P:(tt + 1) * P].bitcast(F32), ALU.subtract), "hid_low")

            ada_n = [0]
            gate_n = [0]

            def ada_rows_out(chunk, b):
                v.wait_ge(S("direct_used"), DNUM[("ada", chunk, 1)] + 1)
                if ada_n[0]:
                    v.wait_ge(S("ada_summed"), ada_n[0])
                st.mark(v.tensor_copy(ada4[:, :], bank[:, b, :]), "ada4_ready")
                ada_n[0] += 1

            def mod_out(chunk, b):
                l, c = chunk
                v.wait_ge(S("ada_summed"), ada_n[0])
                dst = mod[:, l, {0: 0, 1: 1, 3: 2, 4: 3}[c // 2], (c % 2) * 4:(c % 2) * 4 + 4, :]
                bias = ada_bT[:, l * 48 + c * 4:l * 48 + c * 4 + 4].unsqueeze(2).to_broadcast([P, 4, 2])
                st.do(v.tensor_tensor(dst, bank[:, b, 0:8].rearrange("p (k c) -> p k c", c=2), bias, ALU.add),
                      "ada_out")

            def gate_out(chunk, b):
                c0 = (chunk[1] % 2) * 512
                gate_n[0] += 1
                v.wait_ge(S("ada_summed"), ada_n[0])
                v.wait_ge(S("gate_bias"), 32 * ((gate_n[0] + 1) // 2))
                for tt in range(TILES):
                    dst = gate[:, tt, c0:c0 + 512]
                    st.do(v.tensor_tensor(dst, bank[:, b + tt, :], dst, ALU.add), "ada_out")

            def residual():
                for tt in range(TILES):
                    st.mark(v.tensor_tensor(xhat[:, tt, :], cat(bank[:, 2 + 2 * tt:4 + 2 * tt, :]), gate[:, tt, :],
                                            ALU.mult), "res_part")
                for tt in range(TILES):
                    v.wait_ge(S("res_part"), st.n["res_part"] - 1 + tt)
                    st.mark(v.tensor_tensor(x[:, tt, :], x[:, tt, :], xhat[:, tt, :], ALU.add), "residual")

            st.do(v.memset(cond[:, :, :], 0.0), "cleared")
            mean_square(0)
            rms_scale(1)
            v.wait_ge(S("silu_c"), 1)
            st.mark(v.tensor_copy(par[:, :], bank[:, 7, 0:NROWS]), "rows_out")
            st.mark(v.tensor_copy(ada_bT[:, :], bank[:, 6, 0:96]), "rows_out")
            st.do(v.tensor_copy(taps[:, :], bank[:, 6, 96:96 + 248]), "rows_out")
            for j, chunk in enumerate(ADA_FIRST):
                if j:
                    mod_out(ADA_FIRST[j - 1], 7)
                ada_rows_out(chunk, 6)
            mod_out(ADA_FIRST[-1], 7)
            gain_scale(0)
            modulate_context(0)
            named("win", 0, 0)
            hidden_low(0)
            named("win", 0, 1)
            named("win", 2, 0)
            v.wait_ge(S("z0_ready"), 2)
            for tt in range(TILES):
                q = z0[:, tt, 0:Q_LORA]
                k = z0[:, tt, Q_LORA:Q_LORA + KV_LORA]
                st.do(v.tensor_tensor(work[:, 0:Q_LORA], q, q, ALU.mult), "lat_part")
                st.do(v.tensor_reduce(small[:, 8 + tt:9 + tt], work[:, 0:Q_LORA], AX, ALU.add), "lat_part")
                st.do(v.tensor_tensor(work[:, 0:KV_LORA], k, k, ALU.mult), "lat_part")
                st.do(v.tensor_reduce(small[:, 10 + tt:11 + tt], work[:, 0:KV_LORA], AX, ALU.add), "lat_part")
            st.do(v.tensor_scalar(small[:, 0:2], small[:, 8:10], 1.0 / Q_LORA, EPS, ALU.mult, ALU.add), "lat_part")
            st.do(v.tensor_scalar(small[:, 2:4], small[:, 10:12], 1.0 / KV_LORA, EPS, ALU.mult, ALU.add), "ms_ready")
            v.wait_ge(S("rstd_ready"), 2)
            v.wait_ge(S("attn_in"), 80)
            for tt in range(TILES):
                st.do(v.scalar_tensor_tensor(kv_lat[:, tt, :], z0[:, tt, Q_LORA:Q_LORA + KV_LORA],
                                             small[:, 2 + tt:3 + tt], kv_gain[:, :], ALU.mult, ALU.mult),
                      "ckv_ready")
            for tt in range(TILES):
                q = z0[:, tt, 0:Q_LORA]
                st.do(v.tensor_scalar(q, q, small[:, tt:tt + 1], None, ALU.mult), "qlat_ready")
            named("win", 2, 1)
            ada_rows_out(ADA_ATTN[0], 6)
            named("qb")
            mod_out(ADA_ATTN[0], 6)
            v.wait_ge(S("lat_high"), 3)
            for c in range(2):
                st.mark(v.scalar_tensor_tensor(
                    upL[:, 0, c, :].rearrange("p (t n) -> p t n", t=TILES),
                    bank[:, 4, :].rearrange("p (t c n) -> p t c n", t=TILES, c=2)[:, :, c, :],
                    par[:, ROWS["q_a"] + c:ROWS["q_a"] + c + 1],
                    upH[:, 0, c, :].rearrange("p (t n) -> p t n", t=TILES).bitcast(F32),
                    ALU.mult, ALU.subtract), "lat_low")
            st.mark(v.tensor_tensor(upL[:, 1, :, :].rearrange("p c n -> p (c n)")[:, 0:3 * P], bank[:, 5, 0:3 * P],
                                    upH[:, 1, :, :].rearrange("p c n -> p (c n)")[:, 0:3 * P].bitcast(F32),
                                    ALU.subtract), "lat_low")
            named("kvb")
            ada_rows_out(ADA_ATTN[1], 6)
            named("win", 3, 0)

            def heads_in(i):
                dst = heads_raw[:, i % 2]
                if i >= 2:
                    v.wait_ge(S("heads_T"), 2 * (i - 1))
                if i < 2:
                    if i == 0:
                        v.wait_ge(S("q_product"), 1)
                    else:
                        product(v, "qb")
                    src = bank[:, 2 * i:2 * i + 2, 0:4 * QK]
                    st.do(v.tensor_copy(dst.rearrange("p (a h) d -> p a (h d)", a=2), src), "heads_in")
                else:
                    j = i - 2
                    b0 = (4, 0, 2)[j]
                    if j < 2:
                        v.wait_ge(S("kv_product"), j + 1)
                    else:
                        product(v, "kvb")
                    src = cat(bank[:, b0:b0 + 2, :]).rearrange("p (h d) -> p h d", h=HEADS)[:, :, 0:NOPE]
                    st.do(v.tensor_copy(dst[:, :, 0:NOPE], src), "nope_in")
                    kpe = z0[:, j, Q_LORA + KV_LORA:Z0] if j < 2 else kpe_c[:, :]
                    st.do(v.tensor_copy(dst[:, :, NOPE:], kpe.unsqueeze(1).to_broadcast([P, HEADS, ROPE])),
                          "heads_in")

            def heads_norm(i):
                h = heads_raw[:, i % 2]
                v.wait_ge(S("heads_sq"), i + 1)
                st.do(v.tensor_reduce(small[:, 8:16], heads_sq, AX, ALU.add), "heads_part")
                st.do(v.tensor_scalar(small[:, 0:8], small[:, 8:16], 1.0 / QK, EPS, ALU.mult, ALU.add), "ms_ready")
                v.wait_ge(S("rstd_ready"), 3 + i)
                st.do(v.tensor_tensor(h, h, small[:, 0:8].unsqueeze(2).to_broadcast([P, HEADS, QK]), ALU.mult),
                      "heads_part")
                g = (q_gain if i < 2 else k_gain)[:, :].unsqueeze(1).to_broadcast([P, HEADS, QK])
                rotate = i in (1, 3)
                st.do(v.tensor_tensor(h, h, g, ALU.mult), "heads_part" if rotate else "heads_normed")
                if rotate:
                    half = ROPE // 4
                    cos = const[:, C_COS:C_SIN].rearrange("p (h d) -> p h d", h=HEADS)
                    sin = const[:, C_SIN:C_SUM2].rearrange("p (h d) -> p h d", h=HEADS)
                    for axis in range(2):
                        for s in range(2):
                            d0 = (2 * axis + s) * half
                            o0 = (2 * axis + 1 - s) * half
                            st.do(v.tensor_tensor(rope_t[:, :, d0:d0 + half],
                                                  h[:, :, NOPE + o0:NOPE + o0 + half],
                                                  sin[:, :, d0:d0 + half], ALU.mult), "heads_part")
                    st.do(v.tensor_tensor(h[:, :, NOPE:], h[:, :, NOPE:], cos, ALU.mult), "heads_part")
                    st.do(v.tensor_tensor(h[:, :, NOPE:], h[:, :, NOPE:], rope_t[:, :, :], ALU.add), "heads_normed")

            v.wait_ge(S("const_in"), 16)
            heads_in(0)
            heads_norm(0)
            heads_in(1)
            mod_out(ADA_ATTN[1], 6)
            named("win", 3, 1)
            heads_norm(1)
            heads_in(2)
            ada_rows_out(ADA_ATTN[2], 6)
            named("win", 1, 0)
            heads_norm(2)
            mod_out(ADA_ATTN[2], 6)
            heads_in(3)
            named("win", 1, 1)
            ada_rows_out(ADA_ATTN[3], 6)
            heads_norm(3)
            mod_out(ADA_ATTN[3], 6)
            heads_in(4)
            v.wait_ge(S("gc_ready"), 2)
            product(v, "win", 3, 1)
            for tt in range(TILES):
                st.do(v.tensor_tensor(stage[:, 0, tt, :], stage[:, 0, tt, :], bank[:, 4 + tt, :], ALU.mult),
                      "v_ready")
            ada_rows_out(ADA_ATTN[4], 6)
            heads_norm(4)
            mod_out(ADA_ATTN[4], 6)
            st.do(v.memset(vTpad[:, :, :, 0:1], 0.0), "pads")
            st.do(v.memset(vTpad[:, :, :, P + 1:P + 2], 0.0), "pads")
            v.wait_ge(S("sc_T"), 1)
            for tt in range(TILES):
                st.do(v.tensor_copy(vTpad[:, :, tt, 1:P + 1],
                                    bank[:, tt, :].rearrange("p (c n) -> p c n", c=SCC)), "vT_ready")
            ada_rows_out(ADA_ATTN[5], 6)
            v.wait_ge(S("scores"), 1)
            st.do(v.tensor_reduce(small[:, 24:32], cat(bank[:, 0:2, :]).rearrange("p (h n) -> p h n", h=HEADS),
                                  AX, ALU.max), "max_part")
            st.do(v.tensor_scalar(small[:, 24:32], small[:, 24:32], -SCALE, None, ALU.mult), "max_ready")
            mod_out(ADA_ATTN[5], 6)
            v.wait_ge(S("scores"), 2)
            st.do(v.tensor_reduce(small[:, 32:40], cat(bank[:, 2:6, :]).rearrange("p (h n) -> p h n", h=HEADS),
                                  AX, ALU.max), "max_part")
            st.do(v.tensor_scalar(small[:, 32:40], small[:, 32:40], -SCALE, None, ALU.mult), "max_ready")
            ada_rows_out(ADA_ATTN[6], 6)
            v.wait_ge(S("exp_c"), HEADS)
            st.do(v.reciprocal(small[:, 0:8], small[:, 8:16]), "max_part")
            st.do(v.tensor_tensor(prob_c, prob_c, small[:, 0:8].unsqueeze(2).to_broadcast([P, HEADS, P]), ALU.mult),
                  "prob_ready")
            v.wait_ge(S("exp_l"), HEADS)
            st.do(v.reciprocal(small[:, 0:8], small[:, 16:24]), "max_part")
            st.do(v.tensor_tensor(prob_l, prob_l, small[:, 0:8].unsqueeze(2).to_broadcast([P, HEADS, 2 * P]),
                                  ALU.mult), "prob_ready")
            mod_out(ADA_ATTN[6], 6)
            v.wait_ge(S("gbT_ready"), 2)
            for c in range(SCC):
                for j in range(3):
                    w = par[:, ROWS["w_sc"] + j * SCC + c:ROWS["w_sc"] + j * SCC + c + 1]
                    src = vTpad[:, c, :, j:j + P]
                    dst = hid4[:, 4 + c, :, :]
                    if j == 0:
                        st.do(v.tensor_scalar(dst, src, w, None, ALU.mult), "sc_part")
                    else:
                        st.do(v.scalar_tensor_tensor(dst, src, w, dst, ALU.mult, ALU.add), "sc_part")
                if c == 1:
                    ada_rows_out(ADA_ATTN[7], 6)
            st.do(v.tensor_tensor(hid[:, 4:8, :].rearrange("p k n -> p (k n)"),
                                  hid[:, 4:8, :].rearrange("p k n -> p (k n)"),
                                  gbT.rearrange("p c t n -> p (c t n)"), ALU.mult), "sc_gated")
            mod_out(ADA_ATTN[7], 6)
            ada_rows_out(ADA_GATE[0][0], 7)
            for tt in range(TILES):
                v.wait_ge(S("hid_high"), 2 + tt + 1)
                st.mark(v.tensor_tensor(hidL[:, 0:4, tt * P:(tt + 1) * P],
                                        bank[:, 2 + tt, :].rearrange("p (c n) -> p c n", c=4),
                                        hidH[:, 0:4, tt * P:(tt + 1) * P].bitcast(F32), ALU.subtract), "hid_low")
            for tt in range(TILES):
                v.wait_ge(S("hid_high"), 4 + tt + 1)
                st.mark(v.tensor_tensor(hidL[:, 4:8, tt * P:(tt + 1) * P], hid4[:, 4:8, tt, :],
                                        hidH[:, 4:8, tt * P:(tt + 1) * P].bitcast(F32), ALU.subtract), "hid_low")
            named("wo", 0, 0)
            gate_out(ADA_GATE[0][0], 0)
            ada_rows_out(ADA_GATE[0][1], 6)
            named("wo", 0, 1)
            named("wo", 1, 0)
            gate_out(ADA_GATE[0][1], 0)
            named("wo", 1, 1)
            product(v, "wo", 1, 1)
            v.wait_ge(S("hid_low"), 6)
            residual()
            ada_rows_out(ADA_GATE[1][0], 6)
            gain_scale(1)
            mean_square(1)
            named("ffn", "a", 0)
            rms_scale(8)
            named("ffn", "b", 0)
            modulate_context(1)
            hidden_low(6)
            n_units = D_FF // UNIT
            for u in range(n_units):
                if u + 1 < n_units:
                    named("ffn", "a", u + 1)
                for tt in range(TILES):
                    v.wait_ge(S("ffn_silu"), TILES * u + tt + 1)
                    at = act[:, u % 2, tt, :]
                    st.mark(v.tensor_tensor(at, at, bank[:, tt, UNIT:2 * UNIT], ALU.mult), "ffn_act")
                if u == 0:
                    gate_out(ADA_GATE[1][0], 4)
                    ada_rows_out(ADA_GATE[1][1], 7)
                if u == 1:
                    gate_out(ADA_GATE[1][1], 4)
                if u + 1 < n_units:
                    named("ffn", "b", u + 1)
                for w in ([u - 1] if u >= 1 else []) + ([u] if u + 1 == n_units else []):
                    v.wait_ge(S("ffn_high"), w + 1)
                    src = bank[:, 6, :].rearrange("p (t c n) -> p c t n", t=TILES, c=UC)
                    for c in range(UC):
                        st.mark(v.tensor_tensor(upL[:, w % 2, c, :].rearrange("p (t n) -> p t n", t=TILES),
                                                src[:, c],
                                                upH[:, w % 2, c, :].rearrange("p (t n) -> p t n", t=TILES).bitcast(F32),
                                                ALU.subtract), "ffn_low")
                    named("ffn", "d", w)
            product(v, "ffn", "d", n_units - 1)
            residual()
            gain_scale(2)
            mean_square(2)
            named("pw1", "a", 0)
            rms_scale(9)
            named("pw1", "b", 0)
            modulate_context(2)
            hidden_low(8)
            st.do(v.memset(uT[:, :, :, 0:PAD], 0.0), "pads")
            st.do(v.memset(uT[:, :, :, PAD + P:], 0.0), "pads")

            def glu(u):
                v.wait_ge(S("sg_ready"), UC * (u + 1))
                for c in range(UC):
                    k = u * UC + c
                    b = par[:, ROWS["pw1_b"] + k:ROWS["pw1_b"] + k + 1]
                    st.mark(v.scalar_tensor_tensor(uT[:, k, :, PAD:PAD + P], bank[:, 4:6, c * P:(c + 1) * P], b,
                                                   sg[:, c], ALU.add, ALU.mult), "glu_ready")
                v.wait_ge(S("glu_ready"), UC * (u + 1))

            def conv_taps(ks, j0, j1):
                for j in range(j0, j1):
                    for k in ks:
                        dst = hid4[:, k, :, :]
                        src = uT[:, k, :, j:j + P]
                        w = taps[:, j * KT + k:j * KT + k + 1]
                        if j == 0:
                            b = par[:, ROWS["dw_b"] + k:ROWS["dw_b"] + k + 1]
                            st.mark(v.tensor_scalar(dst, src, w, b, ALU.mult, ALU.add), "conv_part")
                        else:
                            v.wait_ge(S("conv_part"), st.n["conv_part"] + 1 - len(ks))
                            st.mark(v.scalar_tensor_tensor(dst, src, w, dst, ALU.mult, ALU.add), "conv_part")

            named("pw1", "a", 1)
            named("pw1", "b", 1)
            named("pw1", "a", 2)
            named("pw1", "b", 2)
            glu(0)
            v.wait_ge(S("hid_low"), 10)
            conv_taps((0, 1), 0, 7)
            named("pw1", "a", 3)
            named("pw1", "b", 3)
            glu(1)
            conv_taps((0, 1), 7, 14)
            glu(2)
            conv_taps((0, 1), 14, 21)
            glu(3)
            conv_taps((0, 1), 21, TAPS)
            rest = tuple(range(2, DVE_TILES))
            ada_rows_out(ADA_CONV[0], 6)
            conv_taps(rest, 0, 6)
            for m in range(1, 4):
                mod_out(ADA_CONV[m - 1], 7)
                ada_rows_out(ADA_CONV[m], 6)
                conv_taps(rest, 6 * m, 6 * m + 6)
            mod_out(ADA_CONV[3], 7)
            ada_rows_out(ADA_GATE[2][0], 6)
            conv_taps(rest, 24, TAPS)
            gate_out(ADA_GATE[2][0], 4)
            ada_rows_out(ADA_GATE[2][1], 6)
            named("pw2", 0, 0)
            gate_out(ADA_GATE[2][1], 4)
            named("pw2", 0, 1)
            named("pw2", 1, 0)
            v.wait_ge(S("ln_sum"), 1)
            st.do(v.tensor_scalar(stat[:, 0, :], bank[:, 0, 0:TILES * P], 1.0 / D, None, ALU.mult), "ln_part")
            st.do(v.tensor_tensor(hid[:, :, :], hid[:, :, :],
                                  stat[:, 0, :].unsqueeze(1).to_broadcast([P, KT, TILES * P]), ALU.subtract),
                  "centred")
            v.wait_ge(S("ln_sum"), 2)
            st.do(v.tensor_scalar(stat[:, 0, :], bank[:, 1, 0:TILES * P], 1.0 / D, EPS, ALU.mult, ALU.add), "ln_part")
            st.do(v.reciprocal(stat[:, 0, :], stat[:, 0, :]), "inv_var")
            v.wait_ge(S("ln_rstd"), 1)
            st.do(v.tensor_tensor(hid[:, :, :], hid[:, :, :],
                                  stat[:, 1, :].unsqueeze(1).to_broadcast([P, KT, TILES * P]), ALU.mult),
                  "ln_scaled")
            v.wait_ge(S("ln_silu"), KT)
            hidden_low(10)
            named("pw2", 1, 1)

            def first_expert(kind, u):
                i = NUM_E[(kind, u)]
                n, m = N_DENSE + i, N_SPLIT + i
                v.wait_ge(S("high_ready"), m + 1)
                v.tensor_tensor(low[:, m % SPLITS, :], raw[:, n % RAWS, :],
                                high[:, m % SPLITS, :].bitcast(F32), ALU.subtract).then_inc(S("low_ready"), 1)

            first_expert("a", 0)
            product(v, "pw2", 1, 1)
            v.wait_ge(S("hid_low"), 12)
            residual()
            ada_rows_out(ADA_GATE[3][0], 6)
            gain_scale(3)
            mean_square(3)
            rms_scale(10)
            first_expert("b", 0)
            modulate_context(3)
            first_expert("a", 1)

            LG, M1, EQ, MASK1, LG2, MASK2, G, M, TMP, POS = range(10)
            r = lambda i: rt[:, i]
            iota8 = const[:, C_IOTA:C_IOTA + EXPERTS].unsqueeze(1).to_broadcast([P, TILES, EXPERTS])

            def wide(c0):
                return small[:, c0:c0 + TILES].unsqueeze(2).to_broadcast([P, TILES, EXPERTS])

            def first_of_max(logits, c_max, c_idx, out):
                st.do(v.tensor_reduce(small[:, c_max:c_max + TILES], r(logits), AX, ALU.max), "route_part")
                st.do(v.tensor_tensor(r(EQ), r(logits), wide(c_max), ALU.is_equal), "route_part")
                st.do(v.scalar_tensor_tensor(r(EQ), r(EQ), -float(EXPERTS), iota8, ALU.mult, ALU.add), "route_part")
                st.do(v.tensor_reduce(small[:, c_idx:c_idx + TILES], r(EQ), AX, ALU.min), "route_part")
                st.do(v.tensor_scalar(small[:, c_idx:c_idx + TILES], small[:, c_idx:c_idx + TILES],
                                      float(EXPERTS), None, ALU.add), "route_part")
                st.do(v.tensor_tensor(r(out), iota8, wide(c_idx), ALU.is_equal), "route_part")

            v.wait_ge(S("logits"), 1)
            st.do(v.tensor_copy(r(LG), bank[:, 6, 0:TILES * EXPERTS].rearrange("p (t e) -> p t e", t=TILES)),
                  "route_part")
            first_of_max(LG, 8, 12, MASK1)
            st.do(v.scalar_tensor_tensor(r(LG2), r(MASK1), -3.0e38, r(LG), ALU.mult, ALU.add), "route_part")
            first_of_max(LG2, 10, 12, MASK2)
            st.do(v.tensor_tensor(small[:, 0:2], small[:, 10:12], small[:, 8:10], ALU.subtract), "top2_diff")
            st.do(v.tensor_tensor(r(M), r(MASK1), r(MASK2), ALU.add), "chosen")
            v.wait_ge(S("top2_exp"), 1)
            st.do(v.tensor_scalar(small[:, 4:6], small[:, 2:4], 1.0, None, ALU.add), "route_part")
            st.do(v.reciprocal(small[:, 4:6], small[:, 4:6]), "route_part")
            st.do(v.tensor_tensor(small[:, 6:8], small[:, 2:4], small[:, 4:6], ALU.mult), "route_part")
            st.do(v.tensor_tensor(r(MASK1), r(MASK1), wide(4), ALU.mult), "route_part")
            st.do(v.tensor_tensor(r(MASK2), r(MASK2), wide(6), ALU.mult), "route_part")
            st.do(v.tensor_tensor(r(G), r(MASK1), r(MASK2), ALU.add), "route_part")
            st.do(v.tensor_copy(route[:, 0:EXPERTS, 2:4].rearrange("p e t -> p t e"), r(G)), "route_part")
            gate_out(ADA_GATE[3][0], 4)
            ada_rows_out(ADA_GATE[3][1], 7)
            v.wait_ge(S("slots"), 1)
            pos = bank[:, 6, 0:TILES * EXPERTS].rearrange("p (t e) -> p t e", t=TILES)
            st.do(v.scalar_tensor_tensor(r(POS), pos, 1.0, r(M), ALU.add, ALU.mult), "route_part")
            st.do(v.tensor_scalar(route[:, 0:EXPERTS, 0:2].rearrange("p e t -> p t e"), r(POS), -1.0, None, ALU.add),
                  "route_part")
            st.do(v.tensor_reduce(small[:, 14:15], bank[:, 6, 16:16 + EXPERTS], AX, ALU.max), "route_part")
            st.do(v.tensor_copy(flag[0:1, 0:1], small[0:1, 14:15]), "flag_ready")

            def tokens_low():
                for tt in range(TILES):
                    v.wait_ge(S("tok_high"), tt + 1)
                    st.mark(v.tensor_tensor(tokL[:, tt, :], cat(bank[:, 2 * tt:2 * tt + 2, :]),
                                            tokH[:, tt, :].bitcast(F32), ALU.subtract), "tok_low")
                v.wait_ge(S("tok_T"), TILES)
                v.wait_ge(S("logits"), 1)
                st.do(v.memset(xhat[:, :, :], 0.0), "y_part")

            def experts(first, split, passes):
                ge = passes * EXPERTS

                def pick_of(e):
                    def count(m):
                        return e * 3 + (3 * ge + m)

                    v.tensor_copy(ecol[:, :], route[:, bass.ds(e, 1), :].rearrange("p a b -> p (a b)")
                                  ).then_inc(S("ecol_ready"), 1)
                    v.wait_ge(S("ecol_ready"), count(1))
                    v.tensor_scalar(ecol[:, 0:2], ecol[:, 0:2], -float(passes * P), None, ALU.add).then_inc(
                        S("ecol_ready"), 1)
                    v.wait_ge(S("ecol_ready"), count(2))
                    v.tensor_scalar(pick[:, 0, :], const[:, C_IOTA:C_IOTA + P], ecol[:, 0:1], None,
                                    ALU.is_equal).then_inc(S("ecol_ready"), 1)
                    v.tensor_scalar(pick[:, 1, :], const[:, C_IOTA:C_IOTA + P], ecol[:, 1:2], None,
                                    ALU.is_equal).then_inc(S("pick_ready"), 1)
                    v.wait_ge(S("pick_ready"), e + (ge + 1))

                def part(e, kind, u):
                    i = NUM_E[(kind, u)]
                    n, m = first + i, split + i
                    v.wait_ge(S("high_ready"), e * PER_E + (m + 1))
                    v.tensor_tensor(low[:, m % SPLITS, :], raw[:, n % RAWS, :],
                                    high[:, m % SPLITS, :].bitcast(F32), ALU.subtract).then_inc(S("low_ready"), 1)

                def up(e, u):
                    v.wait_ge(S("e_silu"), e * UNITS_E + (ge * UNITS_E + u + 1))
                    v.tensor_tensor(eact[:, u % 2, :], eact[:, u % 2, :], bank[:, u % 2, UNIT:2 * UNIT],
                                    ALU.mult).then_inc(S("e_act"), 1)

                def act_low(e, w):
                    v.wait_ge(S("e_high"), e * UNITS_E + (ge * UNITS_E + w + 1))
                    v.tensor_tensor(upL[:, w % 2, :, 0:P],
                                    bank[:, 2 + w % 2, 0:UNIT].rearrange("p (c n) -> p c n", c=UC),
                                    upH[:, w % 2, :, 0:P].bitcast(F32), ALU.subtract).then_inc(S("e_low"), 1)

                def start(e):
                    part(e, "b", 1)
                    up(e, 0)

                def body(e, last):
                    for u in range(1, UNITS_E):
                        if u + 1 < UNITS_E:
                            part(e, "a", u + 1)
                        up(e, u)
                        if u + 1 < UNITS_E:
                            part(e, "b", u + 1)
                        act_low(e, u - 1)
                        part(e, "d", u - 1)
                        if u == 4 and not last:
                            v.wait_ge(S("back_T"), e + (ge + 1))
                            pick_of(e + 1)
                    part(e, "d", UNITS_E - 1)
                    act_low(e, UNITS_E - 1)
                    if not last:
                        part(e + 1, "a", 0)
                        part(e + 1, "b", 0)
                    v.tensor_copy(gcol[:, :], route[:, bass.ds(e, 1), :].rearrange("p a b -> p (a b)")
                                  ).then_inc(S("gcol_ready"), 1)
                    for h in range(2):
                        v.wait_ge(S("out_high"), e * 2 + (2 * ge + h + 1))
                        v.tensor_tensor(outL[:, h * 512:(h + 1) * 512], bank[:, 4 + h, :],
                                        outH[:, h * 512:(h + 1) * 512].bitcast(F32), ALU.subtract).then_inc(
                                            S("out_low"), 1)
                    if not last:
                        part(e + 1, "a", 1)
                        start(e + 1)
                    v.wait_ge(S("gcol_ready"), e + (ge + 1))
                    for tt in range(TILES):
                        for h in range(2):
                            i = 2 * tt + h
                            ys = xhat[:, tt, h * 512:(h + 1) * 512]
                            v.wait_ge(S("scattered"), e * 4 + (4 * ge + i + 1))
                            v.scalar_tensor_tensor(ys, bank[:, 4 + i, :], gcol[:, 2 + tt:3 + tt], ys, ALU.mult,
                                                   ALU.add).then_inc(S("y_part"), 1)
                    v.wait_ge(S("y_part"), e * 4 + (4 * ge + 5))

                pick_of(0)
                if passes:
                    part(0, "a", 0)
                    part(0, "b", 0)
                    part(0, "a", 1)
                else:
                    tokens_low()
                    gate_out(ADA_GATE[3][1], 4)
                start(0)
                with v.Fori(0, EXPERTS - 1) as e:
                    body(e, False)
                body(EXPERTS - 1, True)

            experts(N_DENSE, N_SPLIT, 0)
            most = v.value_load(flag[0:1, 0:1], min_val=0, max_val=TILES * P)
            with v.If(most > P):
                experts(N_DENSE + EXPERTS * PER_E, N_SPLIT + EXPERTS * PER_E, 1)
            for tt in range(TILES):
                st.do(v.tensor_tensor(xhat[:, tt, :], xhat[:, tt, :], gate[:, tt, :], ALU.mult), "y_gated")
                st.do(v.tensor_tensor(x[:, tt, :], x[:, tt, :], xhat[:, tt, :], ALU.add),
                      "y_ready" if tt == 1 else "y_gated")

        @block.tensor
        def _(pe):
            st = Steps(pe)

            def taken(n):
                pe.wait_ge(S("low_ready"), n + 1)

            def mm3(out, xh, xl, wh, wl, start, stop):
                pe.matmul(out, xh, wh, start=start, stop=False)
                pe.matmul(out, xh, wl, start=False, stop=False)
                return pe.matmul(out, xl, wh, start=False, stop=stop)

            ada_n, ada_outs = [0], [0]

            def ada_rows(chunk, b):
                for kh in range(2):
                    m = STREAM[("ada", chunk, kh)]
                    pe.wait_ge(S(f"raw_in{m % RAWS}"), arrived_value(m))
                    for k in range(KH):
                        last = pe.matmul(bank[32 * k:32 * k + 32, b, :], cond[:, kh * KH + k, :],
                                         w_slot(raw, m % RAWS, (KH, 512))[:, k, :], start=kh == 0, stop=kh == 1)
                    last.then_inc(S("direct_used"), 1)

            def ada_read():
                pe.wait_ge(S("ada_out"), ada_outs[0])

            def rows_read():
                pe.wait_ge(S("ada4_ready"), ada_n[0] + 1)

            def mod_sum(b):
                ada_n[0] += 1
                pe.wait_ge(S("ada4_ready"), ada_n[0])
                for k in range(4):
                    last = pe.matmul(bank[:, b, 2 * k:2 * k + 2], ada4[:, k * P:(k + 1) * P],
                                     const[:, C_SUM2:C_SUM2 + 2], start=True, stop=True)
                st.mark(last, "ada_summed")
                ada_outs[0] += 1

            def gate_sum(b):
                ada_n[0] += 1
                pe.wait_ge(S("ada4_ready"), ada_n[0])
                for tt in range(TILES):
                    last = pe.matmul(bank[:, b + tt, :], const[:, C_SUMB + tt * P:C_SUMB + (tt + 1) * P],
                                     ada4[:, :], start=True, stop=True)
                st.mark(last, "ada_summed")
                ada_outs[0] += 2

            def transpose_x(i):
                pe.wait_ge(S("xhat_ready"), 2 * i + 2)
                for tt in range(TILES):
                    for k in range(KT):
                        last = pe.transpose(bank[:, 2 * tt + k // 4, (k % 4) * P:(k % 4 + 1) * P],
                                            xhat[:, tt, k * P:(k + 1) * P], ident)
                st.mark(last, "xhat_T")

            def linear(pieces, cw, out_bank):
                for kh, piece in enumerate(pieces):
                    n = NUM[piece]
                    taken(n)
                    for k in range(KH):
                        kk = kh * KH + k
                        for tt in range(TILES):
                            sl = slice(tt * P, (tt + 1) * P)
                            last = mm3(bank[:, out_bank(tt), 0:cw], hidH[:, kk, sl], hidL[:, kk, sl],
                                       w_slot(high, n % SPLITS, (KH, cw))[:, k, :],
                                       w_slot(low, n % SPLITS, (KH, cw))[:, k, :], kk == 0, kk == KT - 1)
                    last.then_inc(S("piece_used"), 1)
                return n

            pe.wait_ge(S("const_in"), 16)
            pe.wait_ge(S("rows_in"), 16 * 13)
            pe.transpose(bank[:, 7, 0:NROWS], prow[0:NROWS, 0, :], ident[0:NROWS, 0:NROWS])
            pe.transpose(bank[:, 6, 0:96], prow[0:96, 1, :], ident[0:96, 0:96])
            for half in range(2):
                last = pe.transpose(bank[:, 6, 96 + half * 124:96 + (half + 1) * 124], prow[0:124, 2 + half, :],
                                    ident[0:124, 0:124])
            st.mark(last, "rows_T")
            transpose_x(0)
            pe.wait_ge(S("silu_c"), 1)
            pe.wait_ge(S("rows_out"), 3)
            for j, chunk in enumerate(ADA_FIRST):
                if j:
                    rows_read()
                ada_rows(chunk, 6)
                if j:
                    if j > 1:
                        ada_read()
                    mod_sum(7)
            ada_read()
            mod_sum(7)
            pe.wait_ge(S("hid_low"), 2)
            linear([("win", 0, 0), ("win", 0, 1)], Z0, lambda tt: tt)
            linear([("win", 2, 0), ("win", 2, 1)], SC, lambda tt: 2 + tt)
            ada_read()
            ada_rows(ADA_ATTN[0], 6)
            mod_sum(6)
            pe.wait_ge(S("qlat_ready"), 2)
            for tt in range(TILES):
                for c in range(2):
                    pe.transpose(bank[:, 4, (2 * tt + c) * P:(2 * tt + c + 1) * P],
                                 z0[:, tt, c * P:(c + 1) * P], ident)
            pe.wait_ge(S("ckv_ready"), 2)
            for j in range(3):
                last = pe.transpose(bank[:, 5, j * P:(j + 1) * P], kv_lat[:, j, :], ident)
            st.mark(last, "lat_T")
            pe.wait_ge(S("lat_low"), 3)
            pe.wait_ge(S("gc_ready"), 2)
            n = NUM[("qb",)]
            taken(n)
            for tt in range(TILES):
                for hh in range(2):
                    for c in range(2):
                        cols = slice(hh * 4 * QK, (hh + 1) * 4 * QK)
                        sl = slice(tt * P, (tt + 1) * P)
                        last = mm3(bank[:, 2 * tt + hh, 0:4 * QK], upH[:, 0, c, sl], upL[:, 0, c, sl],
                                   w_slot(high, n % SPLITS, (2, HEADS * QK))[:, c, cols],
                                   w_slot(low, n % SPLITS, (2, HEADS * QK))[:, c, cols], c == 0, c == 1)
                if tt == 0:
                    st.mark(last, "q_product")
            last.then_inc(S("piece_used"), 1)
            ada_read()
            ada_rows(ADA_ATTN[1], 6)
            n = NUM[("kvb",)]
            taken(n)
            ckvH = upH[:, 1, :, :].rearrange("p c n -> p (c n)")
            ckvL = upL[:, 1, :, :].rearrange("p c n -> p (c n)")

            def keys_values(j):
                b0 = (4, 0, 2)[j]
                if j:
                    pe.wait_ge(S("heads_in"), j)
                for hh in range(2):
                    last = mm3(bank[:, b0 + hh, :], ckvH[:, j * P:(j + 1) * P], ckvL[:, j * P:(j + 1) * P],
                               high[:, n % SPLITS, hh * 512:(hh + 1) * 512],
                               low[:, n % SPLITS, hh * 512:(hh + 1) * 512], True, True)
                if j < 2:
                    st.mark(last, "kv_product")
                else:
                    last.then_inc(S("piece_used"), 1)

            def heads_transposed(i):
                pe.wait_ge(S("heads_normed"), i + 1)
                for half in range(2):
                    if i or half:
                        pe.wait_ge(S("heads_out"), 2 * i + half)
                    for h in range(4):
                        last = pe.transpose(bank[0:QK, 7, h * P:(h + 1) * P],
                                            heads_raw[:, i % 2, 4 * half + h, :], ident)
                    st.mark(last, "heads_T")

            keys_values(0)
            mod_sum(6)
            heads_transposed(0)
            keys_values(1)
            keys_values(2)
            ada_read()
            ada_rows(ADA_ATTN[2], 6)
            heads_transposed(1)
            mod_sum(6)
            pe.wait_ge(S("heads_in"), 3)
            pe.wait_ge(S("vals_ready"), 1)
            linear([("win", 3, 0), ("win", 3, 1)], SC, lambda tt: 4 + tt)
            heads_transposed(2)
            ada_read()
            ada_rows(ADA_ATTN[3], 6)
            pe.wait_ge(S("heads_in"), 4)
            pe.wait_ge(S("vals_ready"), 2)
            linear([("win", 1, 0), ("win", 1, 1)], SC, lambda tt: tt)
            mod_sum(6)
            heads_transposed(3)
            ada_read()
            ada_rows(ADA_ATTN[4], 6)
            mod_sum(6)
            heads_transposed(4)
            pe.wait_ge(S("v_ready"), 2)
            pe.wait_ge(S("gb_ready"), 2)
            pe.wait_ge(S("heads_in"), 5)
            pe.wait_ge(S("vals_ready"), 3)
            for w in range(2):
                for tt in range(TILES):
                    for c in range(SCC):
                        last = pe.transpose(bank[:, 2 * w + tt, c * P:(c + 1) * P],
                                            stage[:, w, tt, c * P:(c + 1) * P], ident)
            st.mark(last, "sc_T")
            ada_read()
            ada_rows(ADA_ATTN[5], 6)
            pe.wait_ge(S("heads_out"), 10)
            pe.wait_ge(S("vT_ready"), 2)
            for h in range(HEADS):
                last = pe.matmul(bank[:, h // 4, (h % 4) * P:(h % 4 + 1) * P], qT[:, 0, h, :], kT[:, 0, h, :],
                                 start=True, stop=True)
            st.mark(last, "scores")
            mod_sum(6)
            pe.wait_ge(S("gbT_ready"), 2)
            for h in range(HEADS):
                for j, src in enumerate((2, 1)):
                    c0 = (h % 2) * 256 + j * P
                    last = pe.matmul(bank[:, 2 + h // 2, c0:c0 + P], qT[:, 1, h, :], kT[:, src, h, :],
                                     start=True, stop=True)
            st.mark(last, "scores")

            def prob_T(g):
                pe.wait_ge(S("prob_ready"), 1 if g < 2 else 2)
                if g >= 2:
                    pe.wait_ge(S("probT_ready"), g - 1)
                for m in range(4):
                    if g < 2:
                        src = prob_c[:, 4 * g + m, :]
                    else:
                        hh, j = divmod(4 * (g - 2) + m, 2)
                        src = prob_l[:, hh, j * P:(j + 1) * P]
                    last = pe.transpose(bank[:, g % 2, m * P:(m + 1) * P], src, ident)
                st.mark(last, "prob_T")

            def times_values(g):
                pe.wait_ge(S("probT_ready"), g + 1)
                for m in range(4):
                    if g < 2:
                        h, j, tt, kv = 4 * g + m, 0, 0, 0
                        start = stop = True
                    else:
                        h, j = divmod(4 * (g - 2) + m, 2)
                        tt, kv = 1, (2, 1)[j]
                        start, stop = j == 0, j == 1
                    p0 = (h % 2) * VH
                    last = pe.matmul(bank[p0:p0 + VH, 2 + tt, (h // 2) * P:(h // 2 + 1) * P],
                                     vals[:, kv, h, :], probT[:, g % 2, m, :], start=start, stop=stop)
                st.mark(last, "pv_group")

            ada_read()
            ada_rows(ADA_ATTN[6], 6)
            pe.wait_ge(S("exp_c"), HEADS)
            prob_T(0)
            prob_T(1)
            mod_sum(6)
            pe.wait_ge(S("exp_l"), HEADS)
            times_values(0)
            prob_T(2)
            times_values(1)
            prob_T(3)
            times_values(2)
            ada_read()
            ada_rows(ADA_ATTN[7], 6)
            prob_T(4)
            times_values(3)
            prob_T(5)
            times_values(4)
            times_values(5)
            ada_rows(ADA_GATE[0][0], 7)
            mod_sum(6)
            ada_read()
            ada_rows(ADA_GATE[0][1], 6)
            pe.wait_ge(S("probT_ready"), 6)
            gate_sum(0)
            pe.wait_ge(S("hid_low"), 6)
            linear([("wo", 0, 0), ("wo", 0, 1)], 512, lambda tt: 2 + 2 * tt)
            ada_read()
            gate_sum(0)
            linear([("wo", 1, 0), ("wo", 1, 1)], 512, lambda tt: 3 + 2 * tt)
            ada_read()
            ada_rows(ADA_GATE[1][0], 6)
            ada_rows(ADA_GATE[1][1], 7)
            transpose_x(1)
            pe.wait_ge(S("residual"), 2)
            gate_sum(4)
            pe.wait_ge(S("hid_low"), 8)

            def gate_up(u, kh, n):
                taken(n)
                for k in range(KH):
                    kk = kh * KH + k
                    for tt in range(TILES):
                        sl = slice(tt * P, (tt + 1) * P)
                        last = mm3(bank[:, tt, :], hidH[:, kk, sl], hidL[:, kk, sl],
                                   w_slot(high, n % SPLITS, (KH, 512))[:, k, :],
                                   w_slot(low, n % SPLITS, (KH, 512))[:, k, :], kk == 0, kk == KT - 1)
                last.then_inc(S("piece_used"), 1)

            n_units = D_FF // UNIT

            def ffn_T(u):
                pe.wait_ge(S("ffn_act"), TILES * (u + 1))
                if u:
                    pe.wait_ge(S("ffn_low"), UC * u)
                for tt in range(TILES):
                    for c in range(UC):
                        last = pe.transpose(bank[:, 6, (UC * tt + c) * P:(UC * tt + c + 1) * P],
                                            act[:, u % 2, tt, c * P:(c + 1) * P], ident)
                st.mark(last, "ffn_T")

            def ffn_down(u):
                n = NUM[("ffn", "d", u)]
                taken(n)
                pe.wait_ge(S("ffn_low"), UC * (u + 1))
                for c in range(UC):
                    for tt in range(TILES):
                        for h in range(2):
                            sl = slice(tt * P, (tt + 1) * P)
                            last = mm3(bank[:, 2 + 2 * tt + h, :], upH[:, u % 2, c, sl], upL[:, u % 2, c, sl],
                                       w_slot(high, n % SPLITS, (UC, D))[:, c, h * 512:(h + 1) * 512],
                                       w_slot(low, n % SPLITS, (UC, D))[:, c, h * 512:(h + 1) * 512],
                                       u == 0 and c == 0, u == n_units - 1 and c == UC - 1)
                last.then_inc(S("piece_used"), 1)
                return n

            for u in range(n_units):
                if u:
                    pe.wait_ge(S("ffn_act"), TILES * u)
                gate_up(u, 0, NUM[("ffn", "a", u)])
                gate_up(u, 1, NUM[("ffn", "b", u)])
                if u == 1:
                    ada_read()
                    gate_sum(4)
                if u >= 1:
                    ffn_T(u - 1)
                if u == 2:
                    ada_read()
                if u >= 2:
                    ffn_down(u - 2)
            ffn_T(n_units - 1)
            ffn_down(n_units - 2)
            ffn_down(n_units - 1)
            transpose_x(2)
            pe.wait_ge(S("hid_low"), 10)

            def pw1_T(u):
                pe.wait_ge(S("ag_ready"), TILES * (u + 1))
                if u:
                    pe.wait_ge(S("glu_ready"), UC * u)
                else:
                    pe.wait_ge(S("residual"), 4)
                for tt in range(TILES):
                    for j in range(2 * UC):
                        last = pe.transpose(bank[:, 4 + tt, j * P:(j + 1) * P],
                                            ag[:, u % 2, tt, j * P:(j + 1) * P], ident)
                st.mark(last, "pw1_T")

            for u in range(4):
                if u >= 2:
                    pe.wait_ge(S("ag_ready"), TILES * (u - 1))
                for kh in range(2):
                    n = NUM[("pw1", "ab"[kh], u)]
                    taken(n)
                    for k in range(KH):
                        kk = kh * KH + k
                        for tt in range(TILES):
                            sl = slice(tt * P, (tt + 1) * P)
                            last = mm3(bank[:, 2 * (u % 2) + tt, :], hidH[:, kk, sl], hidL[:, kk, sl],
                                       w_slot(high, n % SPLITS, (KH, 512))[:, k, :],
                                       w_slot(low, n % SPLITS, (KH, 512))[:, k, :], kk == 0, kk == KT - 1)
                    last.then_inc(S("piece_used"), 1)
                if u:
                    pw1_T(u - 1)
            pw1_T(3)

            def conv_taps(k, j0, j1):
                if j0 == 0:
                    pe.wait_ge(S("glu_ready"), k + 1)
                    if k >= DVE_TILES + 2:
                        pe.wait_ge(S("conv_pe_ready"), k - DVE_TILES - 1)
                    elif k == DVE_TILES:
                        pe.wait_ge(S("ag_ready"), TILES * 4)
                for j in range(j0, j1):
                    i = (k - DVE_TILES) * TAPS + j
                    pe.wait_ge(S("diag_ready"), i + 1)
                    st.mark(pe.matmul(bank[:, k % 2, 0:TILES * P].rearrange("p (t n) -> p t n", t=TILES),
                                      diag[:, i % DIAGS, :], uT[:, k, :, j:j + P], start=j == 0, stop=j == TAPS - 1),
                            "tap_used")

            ada_read()
            ada_rows(ADA_CONV[0], 6)
            conv_taps(5, 0, 16)
            rows_read()
            ada_rows(ADA_CONV[1], 6)
            mod_sum(7)
            conv_taps(5, 16, TAPS)
            rows_read()
            ada_rows(ADA_CONV[2], 6)
            ada_read()
            mod_sum(7)
            conv_taps(6, 0, 16)
            rows_read()
            ada_rows(ADA_CONV[3], 6)
            ada_read()
            mod_sum(7)
            conv_taps(6, 16, TAPS)
            rows_read()
            ada_rows(ADA_GATE[2][0], 6)
            ada_read()
            mod_sum(7)
            conv_taps(7, 0, 16)
            rows_read()
            ada_rows(ADA_GATE[2][1], 6)
            pe.wait_ge(S("glu_ready"), KT)
            gate_sum(4)
            conv_taps(7, 16, TAPS)
            ada_read()
            gate_sum(4)
            pe.wait_ge(S("conv_pe_ready"), KT - DVE_TILES)
            pe.wait_ge(S("conv_part"), DVE_TILES * TAPS)
            for k in range(KT):
                last = pe.matmul(bank[:, 0, 0:TILES * P], const[:, C_ONES:C_ONES + P], hid[:, k, :],
                                 start=k == 0, stop=k == KT - 1)
            st.mark(last, "ln_sum")
            pe.wait_ge(S("sq_ready"), 1)
            for k in range(KT):
                last = pe.matmul(bank[:, 1, 0:TILES * P], const[:, C_ONES:C_ONES + P], sq[:, k, :],
                                 start=k == 0, stop=k == KT - 1)
            st.mark(last, "ln_sum")
            ada_read()
            pe.wait_ge(S("pw2_bias_in"), 16)
            for tt in range(TILES):
                for h in range(2):
                    pe.matmul(bank[:, 2 + 2 * tt + h, :], const[0:1, C_ONES:C_ONES + P],
                              pw2_b[0:1, h * 512:(h + 1) * 512], start=True, stop=False)
            pe.wait_ge(S("hid_low"), 12)
            for h in range(2):
                for kh in range(2):
                    n = NUM[("pw2", h, kh)]
                    taken(n)
                    for k in range(KH):
                        kk = kh * KH + k
                        for tt in range(TILES):
                            sl = slice(tt * P, (tt + 1) * P)
                            last = mm3(bank[:, 2 + 2 * tt + h, :], hidH[:, kk, sl], hidL[:, kk, sl],
                                       w_slot(high, n % SPLITS, (KH, 512))[:, k, :],
                                       w_slot(low, n % SPLITS, (KH, 512))[:, k, :], False, kk == KT - 1)
                    last.then_inc(S("piece_used"), 1)
            ada_rows(ADA_GATE[3][0], 6)
            ada_rows(ADA_GATE[3][1], 7)
            transpose_x(3)
            pe.wait_ge(S("residual"), 6)
            gate_sum(4)
            pe.wait_ge(S("hid_ctx"), 4)
            pe.wait_ge(S("hid_lat"), 4 * KT)
            pe.wait_ge(S("router_in"), 16)
            for tt in range(TILES):
                for k in range(KT):
                    last = pe.matmul(bank[:, 6, tt * EXPERTS:(tt + 1) * EXPERTS], hid[:, k, tt * P:(tt + 1) * P],
                                     router_w[:, k, :], start=k == 0, stop=k == KT - 1)
            st.mark(last, "logits")
            for tt in range(TILES):
                for k in range(KT):
                    last = pe.transpose(bank[:, 2 * tt + k // 4, (k % 4) * P:(k % 4 + 1) * P],
                                        hid[:, k, tt * P:(tt + 1) * P], ident)
                st.mark(last, "tok_T")
            pe.wait_ge(S("chosen"), 1)
            M = 7
            before = const[:, C_BEFORE:C_BEFORE + P]
            ones = const[:, C_ONES:C_ONES + P]
            pe.matmul(bank[:, 6, 0:EXPERTS], before, rt[:, M, 0], start=True, stop=True)
            pe.matmul(bank[:, 6, EXPERTS:2 * EXPERTS], ones, rt[:, M, 0], start=True, stop=False)
            pe.matmul(bank[:, 6, EXPERTS:2 * EXPERTS], before, rt[:, M, 1], start=False, stop=True)
            pe.matmul(bank[:, 6, 2 * EXPERTS:3 * EXPERTS], ones, rt[:, M, 0], start=True, stop=False)
            st.mark(pe.matmul(bank[:, 6, 2 * EXPERTS:3 * EXPERTS], ones, rt[:, M, 1], start=False, stop=True),
                    "slots")
            ada_read()
            gate_sum(4)
            pe.wait_ge(S("flag_ready"), 1)

            pe.wait_ge(S("ada4_ready"), ada_n[0])

            def experts(first, split, passes):
                ge = passes * EXPERTS

                def gather(e):
                    pe.wait_ge(S("pickR_ready"), e + (ge + 1))
                    for part, src in enumerate((tokH, tokL)):
                        if part:
                            pe.wait_ge(S("tok_low"), TILES)
                        for kh in range(2):
                            for k in range(KH):
                                kk = kh * KH + k
                                for tt in range(TILES):
                                    last = pe.matmul(bank[:, (6, 0)[part] + kh, k * P:(k + 1) * P],
                                                     src[:, tt, kk * P:(kk + 1) * P], pickR[:, tt, :],
                                                     start=tt == 0, stop=tt == TILES - 1)
                            last.then_inc(S("gathered"), 1)

                def ready(e, m):
                    pe.wait_ge(S("low_ready"), e * PER_E + (m + 1))

                def gate_up(e, u):
                    for kh, kind in enumerate("ab"):
                        m = split + NUM_E[(kind, u)]
                        ready(e, m)
                        for k in range(KH):
                            kk = kh * KH + k
                            last = mm3(bank[:, u % 2, :], slotH[:, kk, :], slotL[:, kk, :],
                                       w_slot(high, m % SPLITS, (KH, 512))[:, k, :],
                                       w_slot(low, m % SPLITS, (KH, 512))[:, k, :], kk == 0, kk == KT - 1)
                        last.then_inc(S("piece_used"), 1)

                def gate_up_first(e):
                    pe.wait_ge(S("slot_ready"), e * 4 + (4 * ge + 4))
                    gate_up(e, 0)

                def e_T(e, u):
                    pe.wait_ge(S("e_act"), e * UNITS_E + (ge * UNITS_E + u + 1))
                    if u >= 2:
                        pe.wait_ge(S("e_low"), e * UNITS_E + (ge * UNITS_E + u - 1))
                    for c in range(UC):
                        last = pe.transpose(bank[:, 2 + u % 2, c * P:(c + 1) * P],
                                            eact[:, u % 2, c * P:(c + 1) * P], ident)
                    last.then_inc(S("e_T"), 1)

                def e_down(e, u):
                    m = split + NUM_E[("d", u)]
                    ready(e, m)
                    pe.wait_ge(S("e_low"), e * UNITS_E + (ge * UNITS_E + u + 1))
                    for c in range(UC):
                        for h in range(2):
                            last = mm3(bank[:, 4 + h, :], upH[:, u % 2, c, 0:P], upL[:, u % 2, c, 0:P],
                                       w_slot(high, m % SPLITS, (UC, D))[:, c, h * 512:(h + 1) * 512],
                                       w_slot(low, m % SPLITS, (UC, D))[:, c, h * 512:(h + 1) * 512],
                                       u == 0 and c == 0, u == UNITS_E - 1 and c == UC - 1)
                    last.then_inc(S("piece_used"), 1)

                def body(e, last_expert):
                    for u in range(1, UNITS_E):
                        gate_up(e, u)
                        e_T(e, u - 1)
                        if u == 2:
                            pe.wait_ge(S("y_part"), e * 4 + (4 * ge + 1))
                        if u >= 2:
                            e_down(e, u - 2)
                        if u == 3:
                            for tt in range(TILES):
                                last = pe.transpose(bank[:, 6, tt * P:(tt + 1) * P], pick[:, tt, :], ident)
                            last.then_inc(S("back_T"), 1)
                    e_T(e, UNITS_E - 1)
                    if not last_expert:
                        pe.wait_ge(S("back_ready"), e + (ge + 1))
                        gather(e + 1)
                    e_down(e, UNITS_E - 2)
                    e_down(e, UNITS_E - 1)
                    if not last_expert:
                        gate_up_first(e + 1)
                    pe.wait_ge(S("back_ready"), e + (ge + 1))
                    pe.wait_ge(S("out_low"), e * 2 + (2 * ge + 2))
                    for tt in range(TILES):
                        for h in range(2):
                            b = 4 + 2 * tt + h
                            pe.matmul(bank[:, b, :], backR[:, tt, :], outH[:, h * 512:(h + 1) * 512],
                                      start=True, stop=False)
                            pe.matmul(bank[:, b, :], backR[:, tt, :], outL[:, h * 512:(h + 1) * 512],
                                      start=False, stop=True).then_inc(S("scattered"), 1)

                if passes:
                    pe.wait_ge(S("y_part"), 4 * ge + 1)
                gather(0)
                if not passes:
                    ada_read()
                gate_up_first(0)
                with pe.Fori(0, EXPERTS - 1) as e:
                    body(e, False)
                body(EXPERTS - 1, True)

            experts(N_DENSE, N_SPLIT, 0)
            most = pe.value_load(flag[0:1, 0:1], min_val=0, max_val=TILES * P)
            with pe.If(most > P):
                experts(N_DENSE + EXPERTS * PER_E, N_SPLIT + EXPERTS * PER_E, 1)


NAMES = ["x_prompt", "x_sample", "cache_ckv", "cache_kpe", "c", "c_ctx", "ada_w", "ada_b", "norm_mix", "norm_ffn",
         "w_in", "q_a_norm", "w_qb", "kv_a_norm", "w_kvb", "q_norm", "k_norm", "w_sc", "w_o", "ffn_gu", "ffn_down",
         "conv_pw1", "conv_pw1_b", "conv_dw", "conv_dw_b", "conv_ln_g", "conv_ln_b", "conv_pw2", "conv_pw2_b",
         "router", "moe_gu", "moe_down"]


def constants():
    import numpy as np
    c = np.zeros((P, C_END), np.float32)
    i = np.arange(P)
    c[:, C_ID:C_ID + P] = np.eye(P)
    c[:, C_BEFORE:C_BEFORE + P] = i[:, None] < i[None, :]
    c[:, C_ONES:C_ONES + P] = 1.0
    c[:, C_IOTA:C_IOTA + P] = i[None, :]
    grid_w = 64
    nf = ROPE // 4
    inv = (np.float32(10000.0) ** (-np.arange(nf, dtype=np.float32) / np.float32(nf))).astype(np.float32)
    for axis, pos in enumerate((i // grid_w, i % grid_w)):
        ang = pos[:, None].astype(np.float32) * inv[None, :]
        for s in range(2):
            d0 = (2 * axis + s) * nf
            for h in range(HEADS):
                c[:, C_COS + h * ROPE + d0:C_COS + h * ROPE + d0 + nf] = np.cos(ang)
                c[:, C_SIN + h * ROPE + d0:C_SIN + h * ROPE + d0 + nf] = np.sin(ang) * (-1.0 if s == 0 else 1.0)
    for row in range(P):
        if row % 32 < 2:
            c[row, C_SUM2 + row % 32] = 1.0
            c[row, C_SUMB + (row % 32) * P:C_SUMB + (row % 32 + 1) * P] = 1.0
    return c


def kernel(**inputs):
    import numpy as np
    import concourse.bacc as bacc
    from concourse.bass_utils import run_bass_kernel_spmd

    nc = bacc.Bacc("TRN2", target_bir_lowering=False, num_devices=1)
    arrays = {name: np.ascontiguousarray(inputs[name]) for name in NAMES}
    arrays["table"] = constants()
    t = {name: nc.dram_tensor(name, arr.shape, F32, kind="ExternalInput").ap() for name, arr in arrays.items()}
    shapes = [(1, P, D), (1, P, D), (1, 1, P, KV_LORA), (1, 1, P, ROPE)]
    outs = [nc.dram_tensor(f"out{i}", s, F32, kind="ExternalOutput").ap() for i, s in enumerate(shapes)]
    build(nc, t, outs)
    r = run_bass_kernel_spmd(nc, [arrays], core_ids=[0])
    return tuple(r.results[0][f"out{i}"] for i in range(4))
```
